# Optimizing a Trainium2 kernel written in Bass

```python
import jax, jax.numpy as jnp
from jax import lax
import numpy as np

D_MODEL = 1024
BATCH = 1
SEQ = 256
DEPTH = 1
DEC_BATCH = 1
DEC_SEQ = 64
PAST_LEN = 512

CHUNK = 64
RET_HEADS = 4
RET_DK = 128
RET_DV = 256
RET_QK = RET_HEADS * RET_DK
RET_V = RET_HEADS * RET_DV
CONV_DIM = D_MODEL
CONV_WIDTH = 31
CONV_HIST = CONV_WIDTH - 1
N_GROUPS = 4
EXPERTS_PER_GROUP = 8
TOP_K_INNER = 2
EXPERT_FF = 512
PLE_DIM = 256
LN_EPS = 1e-5
ROPE_BASE = 10000.0
DN_ALPHA = float((2 * DEPTH) ** 0.25)
DN_BETA = float((8 * DEPTH) ** -0.25)
SPLITS = [RET_QK, 2 * RET_QK, 2 * RET_QK + RET_V, 2 * RET_QK + 2 * RET_V,
          2 * RET_QK + 2 * RET_V + 2 * CONV_DIM, 2 * RET_QK + 2 * RET_V + 2 * CONV_DIM + D_MODEL]
IN_COLS = 2 * RET_QK + 2 * RET_V + 2 * CONV_DIM + 2 * D_MODEL

kernel_name = 'retention_conformer_hmoe_stream_step'

def layer_norm(x, g, b):
    xf = x.astype(jnp.float32)
    mu = jnp.mean(xf, axis=-1, keepdims=True)
    var = jnp.mean(jnp.square(xf - mu), axis=-1, keepdims=True)
    return ((xf - mu) * lax.rsqrt(var + LN_EPS) * g.astype(jnp.float32) + b.astype(jnp.float32)).astype(x.dtype)

def log_decay():
    return jnp.log1p(-jnp.exp2(-5.0 - jnp.arange(RET_HEADS, dtype=jnp.float32)))

def rotary(x, pos):
    half = RET_DK // 2
    inv = ROPE_BASE ** (-jnp.arange(half, dtype=jnp.float32) / half)
    ang = pos.astype(jnp.float32)[:, None] * inv[None, :]
    cos = jnp.cos(ang)[:, None, :]
    sin = jnp.sin(ang)[:, None, :]
    x1 = x[..., :half].astype(jnp.float32)
    x2 = x[..., half:].astype(jnp.float32)
    return jnp.concatenate([x1 * cos - x2 * sin, x1 * sin + x2 * cos], axis=-1).astype(x.dtype)

def in_projection(h, pos, w_in):
    B, T, _ = h.shape
    z = h @ w_in
    q, k, v, g, glu, ga, gb = jnp.split(z, SPLITS, axis=-1)
    q = rotary(q.reshape(B, T, RET_HEADS, RET_DK), pos)
    k = rotary(k.reshape(B, T, RET_HEADS, RET_DK), pos) * (RET_DK ** -0.5)
    v = v.reshape(B, T, RET_HEADS, RET_DV)
    return q, k, v, g, glu, ga, gb

def chunk_kv(k, v):
    L = k.shape[-3]
    idx = jnp.arange(L, dtype=jnp.float32)
    zeta = jnp.exp(log_decay()[:, None] * (L - 1.0 - idx)[None, :])
    return jnp.einsum('...lhk,...lhv,hl->...hkv', k, v, zeta)

def chunk_out(q, k, v, r_prev):
    L = q.shape[-3]
    lg = log_decay()
    idx = jnp.arange(L, dtype=jnp.float32)
    dmask = jnp.exp(lg[:, None, None] * jnp.abs(idx[:, None] - idx[None, :]))
    xi = jnp.exp(lg[:, None] * (idx + 1.0)[None, :])
    s = jnp.einsum('...lhk,...mhk->...hlm', q, k) * dmask
    inner = jnp.einsum('...hlm,...mhv->...lhv', s, v)
    cross = jnp.einsum('...lhk,...hkv->...lhv', q, r_prev) * xi.T[:, :, None]
    return inner + cross

def retention_out(o, g, w_ret_out):
    B, T = o.shape[0], o.shape[1]
    of = o.astype(jnp.float32)
    mu = jnp.mean(of, axis=-1, keepdims=True)
    var = jnp.mean(jnp.square(of - mu), axis=-1, keepdims=True)
    on = ((of - mu) * lax.rsqrt(var + LN_EPS)).reshape(B, T, RET_V).astype(g.dtype)
    return (on * jax.nn.silu(g)) @ w_ret_out

def glu_gate(glu):
    return glu[..., :CONV_DIM] * jax.nn.sigmoid(glu[..., CONV_DIM:])

def conv_out(u_pad, conv_w, conv_b, conv_ln_g, conv_ln_b, w_conv_out):
    c = lax.conv_general_dilated(u_pad, conv_w.astype(u_pad.dtype)[:, None, :], window_strides=(1,),
                                 padding='VALID', dimension_numbers=('NWC', 'WIO', 'NWC'),
                                 feature_group_count=CONV_DIM)
    c = jax.nn.silu(layer_norm(c + conv_b, conv_ln_g, conv_ln_b))
    return c @ w_conv_out

def merge(y_ret, y_conv, ga, gb, w_out):
    return (jax.nn.sigmoid(ga) * y_ret + jax.nn.sigmoid(gb) * y_conv) @ w_out

def token_mix_prompt(h, pos, w_in, w_ret_out, conv_w, conv_b, conv_ln_g, conv_ln_b, w_conv_out, w_out):
    B, T, _ = h.shape
    nc = T // CHUNK
    q, k, v, g, glu, ga, gb = in_projection(h, pos, w_in)
    qc = q.reshape(B, nc, CHUNK, RET_HEADS, RET_DK)
    kc = k.reshape(B, nc, CHUNK, RET_HEADS, RET_DK)
    vc = v.reshape(B, nc, CHUNK, RET_HEADS, RET_DV)
    kv = chunk_kv(kc, vc)
    chunk_decay = jnp.exp(log_decay() * CHUNK)[:, None, None]

    def step(r, kv_n):
        return chunk_decay * r + kv_n, r

    r_last, r_prev = lax.scan(step, jnp.zeros_like(kv[:, 0]), jnp.moveaxis(kv, 1, 0))
    o = chunk_out(qc, kc, vc, jnp.moveaxis(r_prev, 0, 1)).reshape(B, T, RET_HEADS, RET_DV)
    y_ret = retention_out(o, g, w_ret_out)
    u = glu_gate(glu)
    u_pad = jnp.pad(u, ((0, 0), (CONV_HIST, 0), (0, 0)))
    y_conv = conv_out(u_pad, conv_w, conv_b, conv_ln_g, conv_ln_b, w_conv_out)
    a = merge(y_ret, y_conv, ga, gb, w_out)
    return a, r_last.astype(h.dtype), u[:, T - CONV_HIST:]

def token_mix_sample(h, pos, r_state, c_state, w_in, w_ret_out, conv_w, conv_b, conv_ln_g, conv_ln_b, w_conv_out, w_out):
    L = h.shape[1]
    q, k, v, g, glu, ga, gb = in_projection(h, pos, w_in)
    o = chunk_out(q, k, v, r_state)
    r_new = jnp.exp(log_decay() * L)[:, None, None] * r_state + chunk_kv(k, v)
    y_ret = retention_out(o, g, w_ret_out)
    u = glu_gate(glu)
    u_pad = jnp.concatenate([c_state.astype(u.dtype), u], axis=1)
    y_conv = conv_out(u_pad, conv_w, conv_b, conv_ln_g, conv_ln_b, w_conv_out)
    a = merge(y_ret, y_conv, ga, gb, w_out)
    return a, r_new.astype(r_state.dtype), u_pad[:, u_pad.shape[1] - CONV_HIST:]

def hier_moe(h, w_rg, b_rg, w_re, b_re, w_eg, w_eu, w_ed):
    hf = h.astype(jnp.float32)
    gprob = jax.nn.softmax(hf @ w_rg.astype(jnp.float32) + b_rg.astype(jnp.float32), axis=-1)
    gp, gi = lax.top_k(gprob, 1)
    elog = jnp.einsum('nd,gde->nge', hf, w_re.astype(jnp.float32)) + b_re.astype(jnp.float32)
    elog = jnp.take_along_axis(elog, gi[:, :, None], axis=1)[:, 0]
    ev, ei = lax.top_k(elog, TOP_K_INNER)
    ew = jax.nn.softmax(ev, axis=-1) * gp
    inner = jnp.sum(jax.nn.one_hot(ei, EXPERTS_PER_GROUP, dtype=jnp.float32) * ew[..., None], axis=1)
    combine = (jax.nn.one_hot(gi[:, 0], N_GROUPS, dtype=jnp.float32)[:, :, None] * inner[:, None, :]).astype(h.dtype)
    out = jnp.zeros_like(h)
    for grp in range(N_GROUPS):
        act = jax.nn.silu(jnp.einsum('nd,edf->nef', h, w_eg[grp])) * jnp.einsum('nd,edf->nef', h, w_eu[grp])
        out = out + jnp.einsum('nef,efd->nd', act * combine[:, grp, :, None], w_ed[grp])
    return out

def channel_block(h, p, w_rg, b_rg, w_re, b_re, w_eg, w_eu, w_ed, w_ple_proj, w_ple_gate, ln2_g, ln2_b):
    B, T, D = h.shape
    m = hier_moe(h.reshape(B * T, D), w_rg, b_rg, w_re, b_re, w_eg, w_eu, w_ed).reshape(B, T, D)
    pe = (p.astype(h.dtype) @ w_ple_proj) * jax.nn.sigmoid(h @ w_ple_gate)
    return layer_norm(DN_ALPHA * h + m + pe, ln2_g, ln2_b)

def setup_inputs(seed: int = 0) -> dict:
    key = jax.random.key(seed)
    ks = jax.random.split(key, 32)

    def nrm(k, shape, scale):
        return jax.random.normal(k, shape, jnp.float32) * scale

    col_scale = np.ones((IN_COLS,), np.float32)
    col_scale[2 * RET_QK:2 * RET_QK + RET_V] = DN_BETA
    w_in = nrm(ks[6], (DEPTH, D_MODEL, IN_COLS), D_MODEL ** -0.5) * jnp.asarray(col_scale)
    return {
        'x_prompt': nrm(ks[0], (BATCH, SEQ, D_MODEL), 1.0),
        'x_sample': nrm(ks[1], (DEC_BATCH, DEC_SEQ, D_MODEL), 1.0),
        'p_prompt': nrm(ks[2], (DEPTH, BATCH, SEQ, PLE_DIM), 1.0),
        'p_sample': nrm(ks[3], (DEPTH, DEC_BATCH, DEC_SEQ, PLE_DIM), 1.0),
        'state_ret': nrm(ks[4], (DEPTH, DEC_BATCH, RET_HEADS, RET_DK, RET_DV), 0.3),
        'state_conv': nrm(ks[5], (DEPTH, DEC_BATCH, CONV_HIST, CONV_DIM), 0.5),
        'ln_in_g': 1.0 + nrm(ks[7], (D_MODEL,), 0.02),
        'ln_in_b': nrm(ks[8], (D_MODEL,), 0.02),
        'w_in': w_in,
        'w_ret_out': nrm(ks[9], (DEPTH, RET_V, D_MODEL), DN_BETA * RET_V ** -0.5),
        'conv_w': nrm(ks[10], (DEPTH, CONV_WIDTH, CONV_DIM), CONV_WIDTH ** -0.5),
        'conv_b': nrm(ks[11], (DEPTH, CONV_DIM), 0.02),
        'conv_ln_g': 1.0 + nrm(ks[12], (DEPTH, CONV_DIM), 0.02),
        'conv_ln_b': nrm(ks[13], (DEPTH, CONV_DIM), 0.02),
        'w_conv_out': nrm(ks[14], (DEPTH, CONV_DIM, D_MODEL), DN_BETA * CONV_DIM ** -0.5),
        'w_out': nrm(ks[15], (DEPTH, D_MODEL, D_MODEL), DN_BETA * D_MODEL ** -0.5),
        'ln1_g': 1.0 + nrm(ks[16], (DEPTH, D_MODEL), 0.02),
        'ln1_b': nrm(ks[17], (DEPTH, D_MODEL), 0.02),
        'w_route_g': nrm(ks[18], (DEPTH, D_MODEL, N_GROUPS), D_MODEL ** -0.5),
        'b_route_g': nrm(ks[19], (DEPTH, N_GROUPS), 0.01),
        'w_route_e': nrm(ks[20], (DEPTH, N_GROUPS, D_MODEL, EXPERTS_PER_GROUP), D_MODEL ** -0.5),
        'b_route_e': nrm(ks[21], (DEPTH, N_GROUPS, EXPERTS_PER_GROUP), 0.01),
        'w_exp_gate': nrm(ks[22], (DEPTH, N_GROUPS, EXPERTS_PER_GROUP, D_MODEL, EXPERT_FF), D_MODEL ** -0.5),
        'w_exp_up': nrm(ks[23], (DEPTH, N_GROUPS, EXPERTS_PER_GROUP, D_MODEL, EXPERT_FF), DN_BETA * D_MODEL ** -0.5),
        'w_exp_down': nrm(ks[24], (DEPTH, N_GROUPS, EXPERTS_PER_GROUP, EXPERT_FF, D_MODEL), DN_BETA * EXPERT_FF ** -0.5),
        'w_ple_proj': nrm(ks[25], (DEPTH, PLE_DIM, D_MODEL), DN_BETA * PLE_DIM ** -0.5),
        'w_ple_gate': nrm(ks[26], (DEPTH, D_MODEL, D_MODEL), D_MODEL ** -0.5),
        'ln2_g': 1.0 + nrm(ks[27], (DEPTH, D_MODEL), 0.02),
        'ln2_b': nrm(ks[28], (DEPTH, D_MODEL), 0.02),
    }

def reference(x_prompt, x_sample, p_prompt, p_sample, state_ret, state_conv,
              ln_in_g, ln_in_b, w_in, w_ret_out, conv_w, conv_b, conv_ln_g, conv_ln_b, w_conv_out, w_out,
              ln1_g, ln1_b, w_route_g, b_route_g, w_route_e, b_route_e, w_exp_gate, w_exp_up, w_exp_down,
              w_ple_proj, w_ple_gate, ln2_g, ln2_b):
    pos_p = jnp.arange(x_prompt.shape[1], dtype=jnp.int32)
    pos_s = PAST_LEN + jnp.arange(x_sample.shape[1], dtype=jnp.int32)
    hp = layer_norm(x_prompt, ln_in_g, ln_in_b)
    hs = layer_norm(x_sample, ln_in_g, ln_in_b)
    ret_p, conv_p, ret_s, conv_s = [], [], [], []
    for i in range(DEPTH):
        a_p, r_p, c_p = token_mix_prompt(hp, pos_p, w_in[i], w_ret_out[i], conv_w[i], conv_b[i],
                                         conv_ln_g[i], conv_ln_b[i], w_conv_out[i], w_out[i])
        a_s, r_s, c_s = token_mix_sample(hs, pos_s, state_ret[i], state_conv[i], w_in[i], w_ret_out[i], conv_w[i],
                                         conv_b[i], conv_ln_g[i], conv_ln_b[i], w_conv_out[i], w_out[i])
        ret_p.append(r_p)
        conv_p.append(c_p)
        ret_s.append(r_s)
        conv_s.append(c_s)
        hp = layer_norm(DN_ALPHA * hp + a_p, ln1_g[i], ln1_b[i])
        hs = layer_norm(DN_ALPHA * hs + a_s, ln1_g[i], ln1_b[i])
        hp = channel_block(hp, p_prompt[i], w_route_g[i], b_route_g[i], w_route_e[i], b_route_e[i], w_exp_gate[i],
                           w_exp_up[i], w_exp_down[i], w_ple_proj[i], w_ple_gate[i], ln2_g[i], ln2_b[i])
        hs = channel_block(hs, p_sample[i], w_route_g[i], b_route_g[i], w_route_e[i], b_route_e[i], w_exp_gate[i],
                           w_exp_up[i], w_exp_down[i], w_ple_proj[i], w_ple_gate[i], ln2_g[i], ln2_b[i])
    new_ret_prompt = jnp.stack(ret_p, axis=0)
    new_conv_prompt = jnp.stack(conv_p, axis=0)
    new_ret_sample = jnp.stack(ret_s, axis=0)
    new_conv_sample = jnp.stack(conv_s, axis=0)
    return (hp, hs, new_ret_prompt, new_conv_prompt, new_ret_sample, new_conv_sample)


_drawn_inputs = setup_inputs


def setup_inputs(seed=0):
    import zlib

    import numpy as np

    out = dict(_drawn_inputs(seed))
    spreads = {}
    factors = {'conv_b': 8.0,
     'conv_ln_g': 8.0,
     'conv_ln_b': 8.0,
     'ln1_g': 2.712,
     'b_route_g': 8.0,
     'b_route_e': 8.0,
     'ln2_g': 3.095,
     'ln2_b': 2.739}
    for name, (base, spread) in spreads.items():
        noise = np.random.default_rng([zlib.crc32(name.encode()), seed]).standard_normal(out[name].shape)
        drawn = base * np.exp(spread * noise) if base else spread * noise
        out[name] = __import__('jax').numpy.asarray(drawn.astype(out[name].dtype))
    for name, factor in factors.items():
        out[name] = (out[name] * factor).astype(out[name].dtype)
    return out
```

```python
import math

import numpy as np

import concourse.bass as bass
from concourse import mybir

D_MODEL, SEQ, DEC_SEQ, PAST_LEN, CHUNK = 1024, 256, 64, 512, 64
TOK = SEQ + DEC_SEQ
TILES = 3
ROWS = [128, 128, 64]
KT = D_MODEL // 128
HEADS, DK, DV = 4, 128, 256
CONV_W = 31
HIST = CONV_W - 1
UCOLS = HIST + SEQ + HIST + DEC_SEQ
CCOLS = UCOLS - HIST
S0 = SEQ + HIST
GROUPS, PER_GROUP = 4, 8
EXPERTS = GROUPS * PER_GROUP
FF = 512
PLE = 256
EPS = 1e-5
ALPHA = 2.0 ** 0.25
SLOTS = 64
ROUNDS = -(-TOK // SLOTS)
BIG = 1e30

CH = 2048
GLU0, QKV0, G0, GA0, RET0, GB0, CONV0, OUT0, PROJ0, GATE0, DENSE = 0, 8, 16, 20, 24, 28, 32, 36, 40, 41, 45
PER_ROUND = 6 * EXPERTS
SPLIT = {0: 0, 1: 1, 3: 2, 4: 3}
RAW_D, RAW_X = 4, 6

C_ID, C_ONES, C_MASK = 0, 128, 256
C_XI = C_MASK + HEADS * 448
C_ZETA = C_XI + HEADS * 64
C_COS = C_ZETA + 12
C_SIN = C_COS + 192
C_IOTA = C_SIN + 192
C_EOFF = C_IOTA + 64
C_PRIO4 = C_EOFF + EXPERTS
C_PRIO8 = C_PRIO4 + 4
C_N = C_PRIO8 + 8
GAMMA = [1.0 - 2.0 ** (-5.0 - h) for h in range(HEADS)]


def _constants():
    c = np.zeros((128, C_N), np.float64)
    p = np.arange(128)
    c[:, C_ID:C_ID + 128] = np.eye(128)
    c[:, C_ONES:C_ONES + 128] = 1.0 / D_MODEL
    scale = DK ** -0.5
    for h, g in enumerate(GAMMA):
        m = C_MASK + 448 * h
        for first, cols in ((0, np.arange(256)), (128, np.arange(128, 256))):
            src, dst = (first + p)[:, None], cols[None, :]
            seen = (dst >= src) | (dst // CHUNK == src // CHUNK)
            c[:, m + 2 * first:m + 2 * first + len(cols)] = np.where(seen, g ** np.abs(dst - src), 0.0) * scale
        l = np.arange(64)
        c[:64, m + 384:m + 448] = g ** np.abs(l[None, :] - l[:, None]) * scale
        c[:, C_XI + 64 * h:C_XI + 64 * (h + 1)] = g ** (l + 1.0)
        for t in range(TILES):
            last = 255 - 128 * t - p if t < 2 else np.maximum(63 - p, 0)
            c[:, C_ZETA + 4 * t + h] = g ** last * scale
    half = DK // 2
    inv = np.float32(10000.0) ** (-np.arange(half, dtype=np.float32) / np.float32(half))
    for t in range(TILES):
        pos = (128 * t + p if t < 2 else PAST_LEN + p % 64).astype(np.float32)
        ang = pos[:, None] * inv[None, :]
        c[:, C_COS + 64 * t:C_COS + 64 * (t + 1)] = np.cos(ang)
        c[:, C_SIN + 64 * t:C_SIN + 64 * (t + 1)] = np.sin(ang)
    c[:, C_IOTA:C_IOTA + 64] = np.arange(64)
    c[:, C_EOFF:C_EOFF + EXPERTS] = SLOTS * np.arange(EXPERTS)
    c[:, C_PRIO4:C_PRIO4 + 4] = 4 - np.arange(4)
    c[:, C_PRIO8:C_PRIO8 + 8] = 8 - np.arange(8)
    return c.astype(np.float32)


class Area:

    def __init__(self, nc, start, size):
        self.nc, self.start, self.next, self.end = nc, start, start, start + size

    def put(self, name, shape, dt, width=4):
        size = -(-int(np.prod(shape[1:])) * width // 32) * 32
        assert self.next + size <= self.end, (name, self.next + size - self.end)
        self.next += size
        return self.nc.alloc_sbuf_tensor_at(name, list(shape), dt, offset=self.next - size)


class Chain:

    def __init__(self, engine, sem):
        self.engine, self.sem, self.n = engine, sem, 0

    def __call__(self, instruction):
        self.n += 1
        instruction.then_inc(self.sem, 1)
        self.engine.wait_ge(self.sem, self.n)


def _program(nc, wstream, x, p_t, state_ret, state_conv, consts, triangle, conv_params, route_w, route_b,
             ln_in, ln1, ln2, y, ret_p, ret_s, conv_p, conv_s):
    F, R, B16 = mybir.dt.float32, mybir.dt.float32r, mybir.dt.bfloat16
    U32, I32 = mybir.dt.uint32, mybir.dt.int32
    ALU, ACT, X = mybir.AluOpType, mybir.ActivationFunctionType, mybir.AxisListType.X
    ds = bass.ds

    y_rows = nc.dram_tensor("y_rows", [ROUNDS * EXPERTS * SLOTS, D_MODEL], F, kind="Internal").ap()

    begin, end = -(-nc.sbuf_base // 32) * 32, nc.sbuf_usable_end // 32 * 32
    sizes = dict(fixed=15168, rows=12288, ring=RAW_D * CH * 4, split=4 * CH * 4, h=20480, u=12160, c=11200,
                 qk=21504, v=24576, g=10240, ga=10240)
    o, spot = begin, {}
    for name, size in sizes.items():
        spot[name] = o
        o += size
    spot["ret"] = o

    def area(name, size=None, skip=0):
        return Area(nc, spot[name] + skip, size if size else sizes[name] - skip)

    a = area("fixed")
    const = a.put("const", [128, C_N], F)
    triu = a.put("triu", [128, 2, 128], B16, 2)
    conv_par = a.put("conv_par", [128, KT, CONV_W + 3], F)
    w_route = a.put("w_route_sb", [128, KT, 36], F)
    b_route = a.put("b_route_sb", [36, 1], F)
    stats = a.put("stats", [128, 6, 6], F)
    mv = a.put("mv", [128, TILES, 2], F)
    rstd = a.put("rstd", [128, TILES], F)
    rows = area("rows").put("rows_sb", [128, TILES, D_MODEL], F)
    raw_d = area("ring").put("raw_dense", [128, RAW_D, CH], F)
    a = area("split")
    whi = a.put("w_hi", [128, 2, CH], R)
    wlo = a.put("w_lo", [128, 2, CH], R)
    a = area("h")
    hT = [a.put("hT_hi", [128, KT, TOK], R), a.put("hT_lo", [128, KT, TOK], R)]
    uT = area("u").put("uT_sb", [128, KT, UCOLS], F)
    cT = area("c").put("cT_sb", [128, KT, CCOLS], F)
    a = area("qk")
    qk = a.put("qk_rows", [128, 2, TILES, 512], F)
    qkT = a.put("qkT", [128, 2, 2, TOK], F)
    rot = a.put("rot", [128, 2, 512], F)
    a = area("v")
    vrow = a.put("v_rows", [128, TILES, D_MODEL], F)
    on = a.put("on_rows", [128, TILES, D_MODEL], F)
    gT = area("g").put("gT", [128, KT, TOK], F)
    sA = area("ga").put("sA", [128, KT, TOK], F)
    a = area("ret", end - spot["ret"])
    rstate = a.put("rstate", [128, HEADS, DV], F)
    sT = a.put("sT", [128, 2, 448], F)
    qx = a.put("qx", [128, 2, 64], F)
    ln_in_gb = area("ga").put("ln_in_gb", [128, 2, D_MODEL], F)
    a = area("g")
    glu_sig = a.put("glu_sig", [128, 2, TOK], F)
    ln_tmp = a.put("ln_tmp", [128, D_MODEL], F)
    ret_out = area("ga").put("ret_out", [128, HEADS, DV], F)
    sB = area("g").put("sB", [128, KT, TOK], F)
    a = area("qk")
    AT = [a.put("AT_hi", [128, KT, TOK], R), a.put("AT_lo", [128, KT, TOK], R)]
    a = area("v")
    CT = [a.put("CT_hi", [128, KT, CCOLS], R), a.put("CT_lo", [128, KT, CCOLS], R)]
    sq = area("u").put("sq", [128, KT, CCOLS], F)
    a = area("h")
    mT = [a.put("m_hi", [128, KT, TOK], R), a.put("m_lo", [128, KT, TOK], R)]
    a = area("ret", end - spot["ret"])
    cstat = a.put("cstat", [128, CCOLS], F)
    at_tmp = Area(nc, spot["ret"] + 4096, 3584).put("at_tmp", [128, 2, TOK], F)
    a = area("h")
    h1T = [a.put("h1T_hi", [128, KT, TOK], R), a.put("h1T_lo", [128, KT, TOK], R)]
    raw_x = [Area(nc, s, CH * 4).put(f"raw_x{i}", [128, CH], F) for i, s in enumerate(
        (spot["u"], spot["u"] + CH * 4, spot["v"], spot["v"] + CH * 4, spot["v"] + 2 * CH * 4, spot["g"]))]
    a = Area(nc, spot["u"] + 2 * CH * 4, spot["v"] - spot["u"] - 2 * CH * 4)
    ln_gb = a.put("ln_gb", [128, 2, D_MODEL], F)
    pT_at = a.next
    pT_raw = a.put("pT_raw", [128, 2, TOK], F)
    pT = [a.put("pT_hi", [128, 2, TOK], R), a.put("pT_lo", [128, 2, TOK], R)]
    h1T_f = Area(nc, a.next, a.end - a.next).put("h1T_f", [128, KT, TOK], F)
    base_rows = a.put("base_rows", [128, TILES, D_MODEL], F)
    a = area("ga", end - spot["ga"])
    h1b = a.put("h1b", [128, 3, TILES, D_MODEL], B16, 2)
    rankm = a.put("rankm", [128, TILES, EXPERTS + 1], F)
    iota = a.put("iota_r", [128, SLOTS], F)
    wts = a.put("wts", [128, 2, TILES], F)
    pos_u = a.put("pos_u", [128, 2, TILES], U32)
    more = a.put("more", [1, 1], I32)
    a = area("g", skip=CH * 4)
    logT = a.put("logT", [36, TOK], F)
    onehot = a.put("onehot", [128, TILES, SLOTS], B16, 2)
    a = area("fixed", 4 * (C_IOTA - C_MASK), skip=4 * C_MASK)
    logit = a.put("logit", [128, TILES, 36], F)
    r4 = a.put("r4", [128, TILES, 4], F)
    gsel = a.put("gsel", [128, TILES, 4], F)
    e32 = a.put("e32", [128, TILES, EXPERTS], F)
    e8 = a.put("e8", [128, 2, TILES, 8], F)
    s8 = a.put("s8", [128, 2, TILES, 8], F)
    r1 = a.put("r1", [128, 12, TILES], F)
    sel = a.put("sel", [128, 2, TILES, EXPERTS], F)
    taken = a.put("taken", [128, TILES, EXPERTS], F)
    taken16 = a.put("taken16", [128, TILES, EXPERTS], B16, 2)
    rank = a.put("rank", [128, TILES + 1, EXPERTS], F)
    wide = a.put("wide_tmp", [128, D_MODEL], F)
    gate_sig = wide[:].rearrange("p (a c) -> p a c", a=2)
    a = area("ring")
    whi_x = [a.put(f"w_hi_x{i}", [128, CH], R) for i in range(2)]
    wlo_x = [a.put(f"w_lo_x{i}", [128, CH], R) for i in range(2)]
    hi_slot = [whi_x[0][:], whi_x[1][:], whi[:, 1, :], whi[:, 0, :]]
    lo_slot = [wlo_x[0][:], wlo_x[1][:], wlo[:, 1, :], wlo[:, 0, :]]
    a = area("h")
    xs = a.put("xs", [128, KT, 2, SLOTS], R)
    gcp = a.put("gate_cp", [64, FF], F)
    gsum = a.put("gate_sum", [64, FF], F)
    gsil = a.put("gate_silu", [64, FF], F)
    usum = a.put("up_sum", [64, FF], F)
    act_rows = a.put("act_rows", [128, FF], F)
    aT = a.put("actT", [128, FF // 128, 2, SLOTS], R)
    ycp = a.put("y_cp", [64, D_MODEL], F)
    a = Area(nc, pT_at, 7680)
    ucp = a.put("up_cp", [64, FF], F)
    ysb = a.put("y_sb", [64, D_MODEL], F)
    yg = area("split").put("y_gathered", [128, 2, TILES, D_MODEL], F)

    ps = nc.alloc_psum_tensor("ps", [128, 8, 512], F)
    ident = const[:, C_ID:C_ID + 128]
    meanw = const[:, C_ONES:C_ONES + 128]

    s = {n: nc.alloc_semaphore(n) for n in (
        "x_in const_in ln_in_in conv_in state_in route_in ln1_in ple_in ln2_in "
        "h_rows hT_psum hT_hi hT_lo hi_ready lo_ready pe_done wide_free row_free sig_ready v_ready qk_rows "
        "heads_T heads_copied kz_ready scores masked kv_ready kv_out o_ready o_read on_ready states_out "
        "onT_psum at_ready at_hi at_lo taps_done mean_ready centred squared var_ready cstd_ready conv_norm "
        "silu_ready ct_hi ct_lo sB_ready m_ready m_hi_ready m_lo_ready out_evac "
        "var_in root_out h1_rows h1T_psum h1T_copied h1T_hi_s h1T_lo_s pT_hi_s pT_lo_s part_hi part_rest part_mid part_last "
        "logT_psum logT_ready logit_psum logit_ready gexp_in gexp eexp_in eexp taken_ready rank_psum rank_read "
        "proj_evac gate_sig_s pe_mul base_ready conv_out1 "
        "onehot_ready x_gathered x_hi x_lo gate_copied gate_summed gate_silued up_copied up_summed act_ready "
        "act_T act_hi act_lo y_copied y_ready y_stored y_free slots_moved pos_ready more_ready y_got final_rows y_out "
        "dve_step act_step pool_step setup").split()}
    raw_d_in = [nc.alloc_semaphore(f"raw_dense_in{i}") for i in range(RAW_D)]
    raw_x_in = [nc.alloc_semaphore(f"raw_expert_in{i}") for i in range(RAW_X)]

    def ss(name):
        return s[name]

    def triple(b):
        return (4, 5, 6) if b % 2 == 0 else (0, 1, 2)

    def chunk_of(r, e, j):
        return DENSE + r * PER_ROUND + (j if isinstance(e, int) and e == 0 else 4 + (e - 1) * 6 + j)

    def split_of(r, e, j):
        return DENSE + r * 4 * EXPERTS + (SPLIT[j] if isinstance(e, int) and e == 0 else 3 + (e - 1) * 4 + SPLIT[j])

    def slot_of(e, j):
        return SPLIT[j] if isinstance(e, int) and e == 0 else (3 + SPLIT[j]) % 4

    def raw_of(e, j):
        if isinstance(e, int) and e == 0:
            return j, 0
        return (4 + j) % 6, (e - 1 if j < 2 else e)

    def round_start(r):
        return DENSE + r * PER_ROUND

    block = nc.Block()
    block.__enter__()

    @block.sync
    def _(sp):
        for t in range(TILES):
            sp.dma_start(rows[0:ROWS[t], t, :], x[128 * t:128 * t + ROWS[t], :]).then_inc(ss("x_in"), 16)
        sp.dma_start(ln_in_gb[:], ln_in.unsqueeze(0).broadcast_to([128, 2, D_MODEL])).then_inc(ss("ln_in_in"), 16)
        sp.dma_start(const[:], consts).then_inc(ss("const_in"), 16)
        sp.dma_start(triu[:], triangle).then_inc(ss("const_in"), 16)
        for i in range(RAW_D):
            sp.dma_start(raw_d[:, i, :], wstream[i]).then_inc(raw_d_in[i], 16)
        with sp.Fori(1, 11) as n:
            for i in range(RAW_D):
                sp.wait_ge(ss("lo_ready"), n * RAW_D + (i - RAW_D + 1))
                sp.dma_start(raw_d[:, i, :], wstream[ds(n * RAW_D + i, 1)].rearrange("a p c -> (a p) c")).then_inc(raw_d_in[i], 16)
        sp.wait_ge(ss("m_ready"), 4)
        for l in range(4):
            sp.dma_start(raw_x[l][:], wstream[DENSE + l]).then_inc(raw_x_in[l], 16)
        for l in range(4, RAW_X):
            sp.dma_start(raw_x[l][:], wstream[DENSE + l]).then_inc(raw_x_in[l], 16)
        sp.wait_ge(ss("lo_ready"), DENSE - RAW_D)
        sp.dma_start(raw_d[:, 0, :], wstream[DENSE - 1]).then_inc(raw_d_in[0], 16)

        def fetch(r, e, j):
            slot = raw_of(e, j)[0]
            sp.dma_start(raw_x[slot][:], wstream[ds(chunk_of(0, e, j), 1)].rearrange("a p c -> (a p) c")).then_inc(raw_x_in[slot], 16)

        def fetch_round(r):
            if not (isinstance(r, int) and r == 0):
                sp.wait_ge(ss("pe_done"), round_start(r))
                for j in range(4):
                    fetch(r, 0, j)
                for j in range(2):
                    fetch(r, 1, j)
            for j in range(2, 6):
                if j - 2 in SPLIT:
                    sp.wait_ge(ss("lo_ready"), split_of(r, 0, j - 2) + 1)
                else:
                    sp.wait_ge(ss("pe_done"), chunk_of(r, 0, j - 2) + 1)
                fetch(r, 1, j)

            def after_same(e, j):
                if j in SPLIT:
                    sp.wait_ge(ss("lo_ready"), split_of(r, e, j) - 3)
                else:
                    sp.wait_ge(ss("pe_done"), chunk_of(r, e, j) - 5)
                fetch(r, e, j)

            with sp.Fori(2, EXPERTS) as e:
                for j in range(6):
                    after_same(e, j)
            for j in range(2):
                after_same(EXPERTS, j)

        fetch_round(0)
        sp.wait_ge(ss("more_ready"), 1)
        flag = sp.value_load(more[0:1, 0:1], min_val=0, max_val=1)
        with sp.If(flag > 0):
            with sp.Fori(1, ROUNDS) as r:
                fetch_round(r)
        for t in range(TILES):
            sp.wait_ge(ss("final_rows"), t + 1)
            sp.dma_start(y[128 * t:128 * t + ROWS[t], :], rows[0:ROWS[t], t, :]).then_inc(ss("y_out"), 16)
        sp.wait_ge(ss("y_out"), 16 * TILES)

    @block.gpsimd
    def _(pool):
        pool.dma_start(conv_par[:], conv_params).then_inc(ss("conv_in"), 16)
        pool.dma_start(uT[:, :, S0:S0 + HIST], state_conv).then_inc(ss("conv_in"), 16)
        pool.dma_start(rstate[:], state_ret.rearrange("h p c -> p h c")).then_inc(ss("state_in"), 16)
        pool.dma_start(w_route[:], route_w).then_inc(ss("route_in"), 16)
        pool.dma_start(b_route[:], route_b).then_inc(ss("route_in"), 16)
        pool.wait_ge(ss("wide_free"), 2 + 8)
        with nc.allow_non_contiguous_dma(reason="thirty columns of each channel"):
            pool.dma_start(conv_p, uT[:, :, HIST + SEQ - HIST:HIST + SEQ]).then_inc(ss("conv_out1"), 16)
            pool.dma_start(conv_s, uT[:, :, UCOLS - HIST:UCOLS]).then_inc(ss("conv_out1"), 16)
        pool.wait_ge(ss("kv_out"), 2 * HEADS)
        pool.dma_start(ret_p.rearrange("h p c -> p h c"), ret_out[:]).then_inc(ss("states_out"), 16)
        pool.dma_start(ret_s.rearrange("h p c -> p h c"), rstate[:]).then_inc(ss("states_out"), 16)
        pool.wait_ge(ss("m_ready"), 4)
        pool.dma_start(ln_gb[:], ln1.unsqueeze(0).broadcast_to([128, 2, D_MODEL])).then_inc(ss("ln1_in"), 16)
        pool.dma_start(pT_raw[:], p_t).then_inc(ss("ple_in"), 16)
        pool.wait_ge(ss("h1_rows"), TILES)
        pool.dma_start(ln_gb[:], ln2.unsqueeze(0).broadcast_to([128, 2, D_MODEL])).then_inc(ss("ln2_in"), 16)

        def store_rows(n):
            pool.wait_ge(ss("y_ready"), n + 1)
            pool.dma_start(y_rows[ds(n * SLOTS, SLOTS), :], ysb[:]).then_inc(ss("y_stored"), 16)
            pool.wait_ge(ss("y_stored"), n * 16 + 16)
            pool.sem_inc(ss("y_free"), 1)

        with pool.Fori(0, EXPERTS) as n:
            store_rows(n)
        def gather_rows(count):
            pool.wait_ge(ss("pos_ready"), 1)
            for t in range(TILES):
                for k in range(2):
                    pool.indirect_dma_start(
                        out=yg[0:ROWS[t], k, t, :], out_offset=None, in_=y_rows[0:count, :],
                        in_offset=bass.IndirectOffsetOnAxis(ap=pos_u[0:ROWS[t], k, t:t + 1], axis=0),
                        bounds_check=count - 1).then_inc(ss("y_got"), 16)

        pool.wait_ge(ss("more_ready"), 1)
        flag = pool.value_load(more[0:1, 0:1], min_val=0, max_val=1)
        with pool.If(flag > 0):
            with pool.Fori(EXPERTS, EXPERTS * ROUNDS) as n:
                store_rows(n)
            gather_rows(ROUNDS * EXPERTS * SLOTS)
        with pool.Else():
            gather_rows(EXPERTS * SLOTS)

    @block.scalar
    def _(act):
        go = nc.scalar.activation

        def hi(i):
            act.wait_ge(raw_d_in[i % RAW_D], 16 * (i // RAW_D + 1))
            if i >= 2:
                act.wait_ge(ss("pe_done"), i - 1)
            go(whi[:, i % 2, :], raw_d[:, i % RAW_D, :], ACT.Copy).then_inc(ss("hi_ready"), 1)

        roots = [0]

        def root():
            roots[0] += 1
            act.wait_ge(ss("var_in"), roots[0])
            go(rstd[:], mv[:, :, 1], ACT.Sqrt).then_inc(ss("root_out"), 1)

        root()
        for k in range(KT):
            act.wait_ge(ss("hT_psum"), k + 1)
            go(hT[0][:, k, :], ps[:, k % 2, 0:TOK], ACT.Copy).then_inc(ss("hT_hi"), 1)

        def head_copies(h):
            act.wait_ge(ss("heads_T"), h + 1)
            for w in range(2):
                go(qkT[:, h % 2, w, :], ps[:, 2 * (h % 2) + w, 0:TOK], ACT.Copy).then_inc(ss("heads_copied"), 1)

        def state_copy(h):
            act.wait_ge(ss("kv_ready"), h + 1)
            go(ret_out[:, h, :], ps[:, 7, 0:DV], ACT.Copy).then_inc(ss("kv_out"), 1)

        for i in range(DENSE):
            hi(i)
            if 1 <= i <= 8:
                act.wait_ge(ss("pe_done"), i)
                go(glu_sig[:, (i - 1) % 2, :], ps[:, 2 * ((i - 1) % 2) + 1, 0:TOK], ACT.Sigmoid).then_inc(ss("sig_ready"), 1)
            if i in (14, 16):
                b = (i - 10) // 2
                act.wait_ge(ss("pe_done"), i)
                for t in range(TILES):
                    go(vrow[0:ROWS[t], t, (b - 2) * 512:(b - 1) * 512], ps[0:ROWS[t], triple(b)[t], :], ACT.Copy).then_inc(ss("v_ready"), 1)
            if i == 16:
                head_copies(0)
                for h in range(HEADS):
                    if h + 1 < HEADS:
                        head_copies(h + 1)
                    state_copy(h)
                    root()
            if 17 <= i <= 20:
                c = i - 1 - G0
                act.wait_ge(ss("pe_done"), i)
                b = 2 * ((i - 1) % 2)
                go(gT[:, 2 * c:2 * c + 2, :], ps[:, b:b + 2, 0:TOK], ACT.Sigmoid).then_inc(ss("sig_ready"), 1)
            if i == 21:
                for v in range(KT):
                    act.wait_ge(ss("at_ready"), v + 1)
                    go(AT[0][:, v, :], at_tmp[:, v % 2, :], ACT.Copy).then_inc(ss("at_hi"), 1)
            if 21 <= i <= 24 or 29 <= i <= 32:
                c, w = (i - 1 - GA0, 12 + i - 1 - GA0) if i <= 24 else (i - 1 - GB0, 20 + i - 1 - GB0)
                act.wait_ge(ss("pe_done"), i)
                act.wait_ge(ss("wide_free"), 2 + w)
                if i == 21:
                    act.wait_ge(ss("states_out"), 32)
                b = 2 * ((i - 1) % 2)
                go((sA if i <= 24 else sB)[:, 2 * c:2 * c + 2, :], ps[:, b:b + 2, 0:TOK], ACT.Sigmoid).then_inc(ss("wide_free"), 1)
            if i == 30:
                act.wait_ge(ss("centred"), 1)
                act.wait_ge(ss("conv_out1"), 32)
                go(sq[:], cT[:], ACT.Square).then_inc(ss("squared"), 1)
            if i == 31:
                act.wait_ge(ss("cstd_ready"), 1)
                go(cstat[:], cstat[:], ACT.Sqrt).then_inc(ss("cstd_ready"), 1)
                act.wait_ge(ss("conv_norm"), 1)
                for j in range(KT):
                    go(cT[:, j, :], cT[:, j, :], ACT.Silu, bias=conv_par[:, j, CONV_W + 2:CONV_W + 3],
                       scale=conv_par[:, j, CONV_W + 1:CONV_W + 2]).then_inc(ss("silu_ready"), 1)
                    act.wait_ge(ss("silu_ready"), j + 1)
                    go(CT[0][:, j, :], cT[:, j, :], ACT.Copy).then_inc(ss("ct_hi"), 1)
            if 33 <= i <= 36:
                c = i - 1 - CONV0
                act.wait_ge(ss("m_ready"), c + 1)
                go(mT[0][:, 2 * c:2 * c + 2, :], sA[:, 2 * c:2 * c + 2, :], ACT.Copy).then_inc(ss("m_hi_ready"), 1)
            if i == 40:
                root()
                for k in range(KT):
                    act.wait_ge(ss("h1T_psum"), k + 1)
                    bank = 3 + 4 * (k % 2)
                    go(h1T_f[:, k, :], ps[:, bank, 0:TOK], ACT.Copy).then_inc(ss("h1T_copied"), 1)
                    go(h1T[0][:, k, :], ps[:, bank, 0:TOK], ACT.Copy).then_inc(ss("h1T_hi_s"), 1)
                act.wait_ge(ss("logT_psum"), 1)
                go(logT[:], ps[0:36, 3, 0:TOK], ACT.Identity, bias=b_route[:]).then_inc(ss("logT_ready"), 1)
                act.wait_ge(ss("gexp_in"), 1)
                go(r4[:], r4[:], ACT.Exp).then_inc(ss("gexp"), 1)
                act.wait_ge(ss("eexp_in"), 1)
                go(r1[:, 5, :], r1[:, 5, :], ACT.Exp).then_inc(ss("eexp"), 1)
                act.wait_ge(ss("h1_rows"), TILES)
                go(h1b[:, 0], rows[:], ACT.Copy).then_inc(ss("part_hi"), 1)
                act.wait_ge(ss("part_rest"), 1)
                go(h1b[:, 1], base_rows[:], ACT.Copy).then_inc(ss("part_mid"), 1)
                act.wait_ge(ss("part_rest"), 2)
                go(h1b[:, 2], base_rows[:], ACT.Copy).then_inc(ss("part_last"), 1)
                act.wait_ge(ss("ple_in"), 16)
                go(pT[0][:], pT_raw[:], ACT.Copy).then_inc(ss("pT_hi_s"), 1)
            if i == 41:
                act.wait_ge(ss("pe_done"), 41)
                act.wait_ge(ss("part_rest"), 2)
                for b in range(2):
                    for t in range(TILES):
                        go(base_rows[0:ROWS[t], t, 512 * b:512 * b + 512], ps[0:ROWS[t], triple(b)[t], :], ACT.Copy).then_inc(ss("proj_evac"), 1)
            if i in (43, 44):
                b = i - 43
                act.wait_ge(ss("pe_done"), 43 + 2 * b)
                for t in range(TILES):
                    n = 3 * b + t
                    if n >= 2:
                        act.wait_ge(ss("pe_mul"), n - 1)
                    go(gate_sig[0:ROWS[t], n % 2, :], ps[0:ROWS[t], triple(b)[t], :], ACT.Sigmoid).then_inc(ss("gate_sig_s"), 1)

        act.wait_ge(ss("lo_ready"), DENSE)

        def hi_x(r, e, j):
            slot, fills = raw_of(e, j)
            act.wait_ge(raw_x_in[slot], (fills + EXPERTS * r) * 16 + 16)
            c = chunk_of(r, e, j)
            if isinstance(e, int) and e == 0:
                act.wait_ge(ss("pe_done"), round_start(r) - (1 if isinstance(r, int) else 0))
            elif isinstance(e, int) and e == 1 and j == 0:
                act.wait_ge(ss("pe_done"), round_start(r))
            elif isinstance(e, int) and e == 1:
                act.wait_ge(ss("pe_done"), chunk_of(r, 0, {1: 0, 3: 1, 4: 3}[j]) + 1)
            else:
                act.wait_ge(ss("pe_done"), c - 5)
            go(hi_slot[slot_of(e, j)], raw_x[slot][:], ACT.Copy).then_inc(ss("hi_ready"), 1)

        def x_high(n, done):
            act.wait_ge(ss("x_gathered"), n + 1)
            act.wait_ge(ss("pe_done"), done)
            go(xs[:, :, 0, :], ps[:, 0, :].rearrange("p (k s) -> p k s", k=KT), ACT.Copy).then_inc(ss("x_hi"), 1)

        def act_high(n):
            act.wait_ge(ss("act_T"), n + 1)
            go(aT[:, :, 0, :], ps[:, 3, :].rearrange("p (k s) -> p k s", k=4)[:, :, 0:SLOTS], ACT.Copy).then_inc(ss("act_hi"), 1)

        def y_copy(done):
            act.wait_ge(ss("pe_done"), done)
            go(ycp[:], ps[64:128, 4:6, :].rearrange("p a c -> p (a c)"), ACT.Copy).then_inc(ss("y_copied"), 1)

        def expert(r, e, first=False, second=False, last=False):
            n = r * EXPERTS + e
            c0 = chunk_of(r, e, 0)
            hi_x(r, e, 0)
            hi_x(r, e, 1)
            if first:
                x_high(n, round_start(r))
            else:
                if not second:
                    y_copy(c0)
                act_high(n - 1)
            hi_x(r, e, 3)
            act.wait_ge(ss("pe_done"), c0 + 2)
            go(gcp[:], ps[64:128, 1, :], ACT.Copy).then_inc(ss("gate_copied"), 1)
            if not first:
                hi_x(r, e, 4)
            act.wait_ge(ss("gate_summed"), n + 1)
            go(gsil[:], gsum[:], ACT.Silu).then_inc(ss("gate_silued"), 1)
            act.wait_ge(ss("pe_done"), c0 + 4)
            go(ucp[:], ps[64:128, 2, :], ACT.Copy).then_inc(ss("up_copied"), 1)
            if not last:
                x_high(n + 1, c0 + 4)

        def rounds(r):
            expert(r, 0, first=True)
            expert(r, 1, second=True)
            with act.Fori(2, EXPERTS - 1) as e:
                expert(r, e)
            expert(r, EXPERTS - 1, last=True)
            hi_x(r, EXPERTS, 0)
            c0 = chunk_of(r, EXPERTS, 0)
            y_copy(c0)
            act_high(r * EXPERTS + EXPERTS - 1)
            act.wait_ge(ss("y_ready"), r * EXPERTS + EXPERTS - 1)
            y_copy(c0 + 2)

        rounds(0)
        act.wait_ge(ss("more_ready"), 1)
        flag = act.value_load(more[0:1, 0:1], min_val=0, max_val=1)
        with act.If(flag > 0):
            with act.Fori(1, ROUNDS) as r:
                rounds(r)
        root()

    @block.vector
    def _(dve):
        V = nc.vector
        tt, stt, ts = V.tensor_tensor, V.scalar_tensor_tensor, V.tensor_scalar
        link = Chain(dve, ss("dve_step"))

        def lo(i):
            dve.wait_ge(ss("hi_ready"), i + 1)
            tt(wlo[:, i % 2, :], raw_d[:, i % RAW_D, :], whi[:, i % 2, :].bitcast(F), ALU.subtract).then_inc(ss("lo_ready"), 1)

        roots = [0]

        def rows_norm(gb, out_sem, out=lambda t: rows[0:ROWS[t], t, :], tmp=ln_tmp):
            for t in range(TILES):
                q = ROWS[t]
                for c in range(2):
                    link(V.bn_stats(stats[0:q, c, :], rows[0:q, t, 512 * c:512 * c + 512]))
                link(V.bn_aggr(mv[0:q, t, :], stats[0:q, 0:2, :]))
            eps_root()
            for t in range(TILES):
                q = ROWS[t]
                link(stt(out=tmp[0:q, :], in0=rows[0:q, t, :], scalar=mv[0:q, t, 0:1], in1=gb[0:q, 0, :],
                         op0=ALU.subtract, op1=ALU.mult))
                stt(out=out(t), in0=tmp[0:q, :], scalar=rstd[0:q, t:t + 1], in1=gb[0:q, 1, :],
                    op0=ALU.mult, op1=ALU.add).then_inc(ss(out_sem), 1)
                if t + 1 < TILES:
                    dve.wait_ge(ss(out_sem), t + 1)

        def eps_root():
            roots[0] += 1
            ts(mv[:, :, 1], mv[:, :, 1], EPS, None, ALU.add).then_inc(ss("var_in"), 1)
            dve.wait_ge(ss("root_out"), roots[0])
            link(V.reciprocal(rstd[:], rstd[:]))

        V.memset(uT[:, :, 0:HIST], 0.0).then_inc(ss("row_free"), 6)
        V.memset(rows[64:128, 2, :], 0.0).then_inc(ss("wide_free"), 2)
        V.memset(rstd[:], 1.0).then_inc(ss("y_free"), 1)
        link(V.memset(mv[:], 1.0))
        dve.wait_ge(ss("x_in"), 16 * TILES)
        dve.wait_ge(ss("ln_in_in"), 16)
        rows_norm(ln_in_gb, "h_rows")
        for k in range(KT):
            dve.wait_ge(ss("hT_hi"), k + 1)
            tt(hT[1][:, k, :], ps[:, k % 2, 0:TOK], hT[0][:, k, :].bitcast(F), ALU.subtract).then_inc(ss("hT_lo"), 1)
        dve.wait_ge(ss("conv_in"), 32)
        dve.wait_ge(ss("const_in"), 32)

        taps = [(j, k) for j in range(KT) for k in range(CONV_W)]

        def conv(count):
            for j, k in taps[:count]:
                src, w = uT[:, j, k:k + CCOLS], conv_par[:, j, k:k + 1]
                if k == 0:
                    i = ts(cT[:, j, :], src, w, conv_par[:, j, CONV_W:CONV_W + 1], ALU.mult, ALU.add)
                else:
                    i = stt(out=cT[:, j, :], in0=src, scalar=w, in1=cT[:, j, :], op0=ALU.mult, op1=ALU.add)
                i.then_inc(ss("taps_done"), 1)
                dve.wait_ge(ss("taps_done"), j * CONV_W + k + 1)
            del taps[:count]

        def rotary(w, t):
            q, bank = ROWS[t], triple(w)[t]
            src = ps[0:q, bank, :].rearrange("p (h a d) -> p h a d", h=HEADS, a=2)
            cos = const[0:q, C_COS + 64 * t:C_COS + 64 * t + 64]
            sin = const[0:q, C_SIN + 64 * t:C_SIN + 64 * t + 64].unsqueeze(1).broadcast_to([q, HEADS, 64])
            cos8 = cos.unsqueeze(1).broadcast_to([q, 2 * HEADS, 64])
            A = rot[0:q, 0, :].rearrange("p (h a d) -> p h a d", h=HEADS, a=2)
            Bv = rot[0:q, 1, :].rearrange("p (h a d) -> p h a d", h=HEADS, a=2)
            out = qk[0:q, w, t, :].rearrange("p (h a d) -> p h a d", h=HEADS, a=2)
            tt(rot[0:q, 0, :].rearrange("p (g d) -> p g d", d=64), ps[0:q, bank, :].rearrange("p (g d) -> p g d", d=64), cos8, ALU.mult).then_inc(ss("dve_step"), 1)
            tt(Bv[:, :, 0, :], src[:, :, 1, :], sin, ALU.mult).then_inc(ss("dve_step"), 1)
            link.n += 2
            tt(Bv[:, :, 1, :], src[:, :, 0, :], sin, ALU.mult).then_inc(ss("row_free"), 1)
            dve.wait_ge(ss("dve_step"), link.n)
            dve.wait_ge(ss("row_free"), 6 + TILES * w + t + 1)
            tt(out[:, :, 0, :], A[:, :, 0, :], Bv[:, :, 0, :], ALU.subtract).then_inc(ss("qk_rows"), 1)
            tt(out[:, :, 1, :], A[:, :, 1, :], Bv[:, :, 1, :], ALU.add).then_inc(ss("qk_rows"), 1)
            dve.wait_ge(ss("qk_rows"), 2 * (TILES * w + t + 1))

        def head_scores(h):
            dve.wait_ge(ss("heads_T"), h + 1)
            for t in range(TILES):
                kr = qk[0:ROWS[t], 1, t, h * DK:(h + 1) * DK]
                ts(kr, kr, const[0:ROWS[t], C_ZETA + 4 * t + h:C_ZETA + 4 * t + h + 1], None, ALU.mult).then_inc(ss("kz_ready"), 1)
            dve.wait_ge(ss("heads_copied"), 2 * h + 1)
            tt(qx[:, h % 2, :], qkT[:, h % 2, 0, 256:320], const[:, C_XI + 64 * h:C_XI + 64 * h + 64], ALU.mult).then_inc(ss("masked"), 1)
            dve.wait_ge(ss("scores"), h + 1)
            m = C_MASK + 448 * h
            tt(sT[:, h % 2, 0:384], ps[:, 4, 0:384], const[:, m:m + 384], ALU.mult).then_inc(ss("masked"), 1)
            tt(sT[0:64, h % 2, 384:448], ps[0:64, 4, 384:448], const[0:64, m + 384:m + 448], ALU.mult).then_inc(ss("masked"), 1)

        def head_norm(h):
            dve.wait_ge(ss("o_ready"), h + 1)
            o = [ps[:, 5, 0:DV], ps[:, 5, DV:2 * DV], ps[0:64, 6, 0:DV]]
            for t in range(TILES):
                link(V.bn_stats(stats[0:ROWS[t], t, :], o[t]))
                link(V.bn_aggr(mv[0:ROWS[t], t, :], stats[0:ROWS[t], t:t + 1, :]))
            dve.wait_ge(ss("kv_out"), 2 * h + 1)
            stt(out=rstate[:, h, :], in0=rstate[:, h, :], scalar=float(GAMMA[h] ** CHUNK), in1=ps[:, 7, DV:2 * DV],
                op0=ALU.mult, op1=ALU.add).then_inc(ss("kv_out"), 1)
            eps_root()
            for t in range(TILES):
                ts(on[0:ROWS[t], t, h * DV:(h + 1) * DV], o[t], mv[0:ROWS[t], t, 0:1], rstd[0:ROWS[t], t:t + 1],
                   ALU.subtract, ALU.mult).then_inc(ss("on_ready"), 1)

        def at_part(v):
            dve.wait_ge(ss("onT_psum"), v + 1)
            tt(at_tmp[:, v % 2, :], ps[:, 5 + v % 2, 0:TOK], gT[:, v, :], ALU.mult).then_inc(ss("at_ready"), 1)
            dve.wait_ge(ss("at_hi"), v + 1)
            tt(AT[1][:, v, :], at_tmp[:, v % 2, :], AT[0][:, v, :].bitcast(F), ALU.subtract).then_inc(ss("at_lo"), 1)

        def bc(ap, shape):
            return ap.broadcast_to(shape)

        def first_max(values, prio, out, width, at_max):
            shape = [128, TILES, width]
            link(stt(out=out, in0=values, scalar=0.0, in1=bc(prio.unsqueeze(1), shape), op0=ALU.is_ge, op1=ALU.mult))
            link(V.tensor_reduce(r1[:, at_max, :], out, X, ALU.max))
            link(tt(out, out, bc(r1[:, at_max, :].unsqueeze(2), shape), ALU.is_equal))

        def route():
            red = V.tensor_reduce
            link(V.memset(logit[64:128, 2, :], 0.0))
            dve.wait_ge(ss("logit_psum"), 1)
            for t in range(TILES):
                link(V.tensor_copy(logit[0:ROWS[t], t, :], ps[0:ROWS[t], 7, 36 * t:36 * t + 36]))
            gl = logit[:, :, 0:GROUPS]
            link(red(r1[:, 0, :], gl, X, ALU.max))
            link(tt(r4[:], gl, bc(r1[:, 0, :].unsqueeze(2), [128, TILES, GROUPS]), ALU.subtract))
            first_max(r4[:], const[:, C_PRIO4:C_PRIO4 + 4], gsel[:], GROUPS, 1)
            V.memset(rankm[:, :, EXPERTS:EXPERTS + 1], -1.0).then_inc(ss("gexp_in"), 1)
            el = logit[:, :, GROUPS:].rearrange("p t (g e) -> p t g e", g=GROUPS)
            four = [128, TILES, GROUPS, PER_GROUP]

            def by_group(ap):
                return ap.rearrange("p t (g e) -> p t g e", g=GROUPS)

            gsel4 = bc(gsel[:].unsqueeze(3), four)
            link(tt(by_group(e32[:]), el, gsel4, ALU.mult))
            link(red(e8[:, 0], e32[:].rearrange("p t (g e) -> p t e g", g=GROUPS), X, ALU.add))
            eight = [128, TILES, PER_GROUP]
            link(red(r1[:, 3, :], e8[:, 0], X, ALU.max))
            link(tt(e8[:, 1], e8[:, 0], bc(r1[:, 3, :].unsqueeze(2), eight), ALU.subtract))
            first_max(e8[:, 1], const[:, C_PRIO8:C_PRIO8 + 8], s8[:, 0], PER_GROUP, 4)
            link(stt(out=e8[:, 1], in0=s8[:, 0], scalar=-BIG, in1=e8[:, 0], op0=ALU.mult, op1=ALU.add))
            link(red(r1[:, 6, :], e8[:, 1], X, ALU.max))
            tt(r1[:, 5, :], r1[:, 6, :], r1[:, 3, :], ALU.subtract).then_inc(ss("eexp_in"), 1)
            link(tt(e8[:, 0], e8[:, 1], bc(r1[:, 6, :].unsqueeze(2), eight), ALU.subtract))
            first_max(e8[:, 0], const[:, C_PRIO8:C_PRIO8 + 8], s8[:, 1], PER_GROUP, 7)
            for k in range(2):
                link(tt(by_group(sel[:, k]), gsel4, bc(s8[:, k].unsqueeze(2), four), ALU.mult))
            link(V.memset(sel[64:128, :, 2, :], 0.0))
            link(tt(taken[:], sel[:, 0], sel[:, 1], ALU.add))
            V.tensor_copy(taken16[:], taken[:]).then_inc(ss("taken_ready"), 1)
            dve.wait_ge(ss("gexp"), 1)
            link(red(r1[:, 2, :], r4[:], X, ALU.add))
            link(V.reciprocal(r1[:, 2, :], r1[:, 2, :]))
            dve.wait_ge(ss("eexp"), 1)
            link(ts(r1[:, 8, :], r1[:, 5, :], 1.0, None, ALU.add))
            link(V.reciprocal(r1[:, 8, :], r1[:, 8, :]))
            link(tt(wts[:, 0, :], r1[:, 8, :], r1[:, 2, :], ALU.mult))
            link(tt(wts[:, 1, :], wts[:, 0, :], r1[:, 5, :], ALU.mult))
            link(V.tensor_copy(iota[:], const[:, C_IOTA:C_IOTA + 64]))
            dve.wait_ge(ss("rank_psum"), 1)
            link(V.tensor_copy(rank[:], ps[:, 7, 128:256].rearrange("p (t e) -> p t e", e=EXPERTS)))
            rk = rank[:, 0:TILES, :]
            link(stt(out=rankm[:, :, 0:EXPERTS], in0=rk, scalar=1.0, in1=taken[:], op0=ALU.add, op1=ALU.mult))
            link(ts(rankm[:, :, 0:EXPERTS], rankm[:, :, 0:EXPERTS], -1.0, None, ALU.add))
            pick(0, 0)
            link(ts(e32[:], rk, float(SLOTS), None, ALU.is_ge))
            for j in range(2, ROUNDS):
                link(stt(out=e32[:], in0=rk, scalar=float(SLOTS * j), in1=e32[:], op0=ALU.is_ge, op1=ALU.add))
            link(stt(out=e32[:], in0=e32[:], scalar=float((EXPERTS - 1) * SLOTS), in1=rk, op0=ALU.mult, op1=ALU.add))
            link(tt(e32[:], e32[:], bc(const[:, C_EOFF:C_EOFF + EXPERTS].unsqueeze(1), [128, TILES, EXPERTS]), ALU.add))
            for k in range(2):
                link(tt(taken[:], sel[:, k], e32[:], ALU.mult))
                link(red(r1[:, 9 + k, :], taken[:], X, ALU.add))
            V.tensor_copy(pos_u[:], r1[:, 9:11, :]).then_inc(ss("pos_ready"), 1)
            link(red(r1[0:1, 11, 0:1], rank[0:1, TILES, :], X, ALU.max))
            ts(more[:], r1[0:1, 11, 0:1], float(SLOTS), None, ALU.is_gt).then_inc(ss("more_ready"), 1)
            dve.wait_ge(ss("part_hi"), 1)
            tt(base_rows[:], rows[:], h1b[:, 0], ALU.subtract).then_inc(ss("part_rest"), 1)
            dve.wait_ge(ss("part_mid"), 1)
            tt(base_rows[:], base_rows[:], h1b[:, 1], ALU.subtract).then_inc(ss("part_rest"), 1)
            dve.wait_ge(ss("pT_hi_s"), 1)
            tt(pT[1][:], pT_raw[:], pT[0][:].bitcast(F), ALU.subtract).then_inc(ss("pT_lo_s"), 1)

        def gates(b):
            for t in range(TILES):
                n = 3 * b + t
                q = ROWS[t]
                dve.wait_ge(ss("gate_sig_s"), n + 1)
                br = base_rows[0:q, t, 512 * b:512 * b + 512]
                tt(br, br, gate_sig[0:q, n % 2, :], ALU.mult).then_inc(ss("pe_mul"), 1)

        def pick(r, e):
            tt(onehot[:], iota[:].unsqueeze(1).broadcast_to([128, TILES, SLOTS]),
               rankm[:, :, ds(e, 1)].broadcast_to([128, TILES, SLOTS]), ALU.is_equal).then_inc(ss("onehot_ready"), 1)

        for i in range(DENSE):
            lo(i)
            b = 2 * ((i - 1) % 2)
            if 1 <= i <= 8:
                dve.wait_ge(ss("sig_ready"), i)
                j = i - 1
                tt(uT[:, j, HIST:HIST + SEQ], ps[:, b, 0:SEQ], glu_sig[:, j % 2, 0:SEQ], ALU.mult).then_inc(ss("dve_step"), 1)
                link.n += 1
                tt(uT[:, j, S0 + HIST:UCOLS], ps[:, b, SEQ:TOK], glu_sig[:, j % 2, SEQ:TOK], ALU.mult).then_inc(ss("wide_free"), 1)
                dve.wait_ge(ss("dve_step"), link.n)
                dve.wait_ge(ss("wide_free"), 2 + i)
            if i in (10, 12):
                dve.wait_ge(ss("pe_done"), i)
                for t in range(TILES):
                    rotary((i - 10) // 2, t)
            if i == 16:
                for h in range(HEADS):
                    head_scores(h)
                    head_norm(h)
            if 17 <= i <= 20:
                c = i - 1 - G0
                dve.wait_ge(ss("sig_ready"), 8 + c + 1)
                tt(gT[:, 2 * c:2 * c + 2, :], ps[:, b:b + 2, 0:TOK], gT[:, 2 * c:2 * c + 2, :], ALU.mult).then_inc(ss("wide_free"), 1)
            if i == 21:
                dve.wait_ge(ss("wide_free"), 2 + 12)
                for v in range(KT):
                    at_part(v)
            if 25 <= i <= 28:
                c = i - 1 - RET0
                dve.wait_ge(ss("pe_done"), i)
                dve.wait_ge(ss("wide_free"), 2 + 16 + c)
                tt(sA[:, 2 * c:2 * c + 2, :], ps[:, b:b + 2, 0:TOK], sA[:, 2 * c:2 * c + 2, :], ALU.mult).then_inc(ss("wide_free"), 1)
            if 1 <= i <= 27 and i != 16:
                conv(10)
            if i == 29:
                conv(len(taps))
                dve.wait_ge(ss("mean_ready"), 1)
                tt(cT[:], cT[:], ps[:, 7, 0:CCOLS].unsqueeze(1).broadcast_to([128, KT, CCOLS]), ALU.subtract).then_inc(ss("centred"), 1)
            if i == 30:
                dve.wait_ge(ss("var_ready"), 1)
                dve.wait_ge(ss("states_out"), 32)
                ts(cstat[:], ps[:, 7, 0:CCOLS], EPS, None, ALU.add).then_inc(ss("cstd_ready"), 1)
            if i == 31:
                dve.wait_ge(ss("cstd_ready"), 2)
                link(V.reciprocal(cstat[:], cstat[:]))
                tt(cT[:], cT[:], cstat[:].unsqueeze(1).broadcast_to([128, KT, CCOLS]), ALU.mult).then_inc(ss("conv_norm"), 1)
                for j in range(KT):
                    dve.wait_ge(ss("ct_hi"), j + 1)
                    tt(CT[1][:, j, :], cT[:, j, :], CT[0][:, j, :].bitcast(F), ALU.subtract).then_inc(ss("ct_lo"), 1)
            if 33 <= i <= 36:
                c = i - 1 - CONV0
                dve.wait_ge(ss("pe_done"), i)
                dve.wait_ge(ss("wide_free"), 2 + 24 + c)
                g = sB[:, 2 * c:2 * c + 2, :]
                tt(g[:, :, 0:SEQ], ps[:, b:b + 2, 0:SEQ], g[:, :, 0:SEQ], ALU.mult).then_inc(ss("dve_step"), 1)
                link.n += 1
                tt(g[:, :, SEQ:TOK], ps[:, b:b + 2, S0:CCOLS], g[:, :, SEQ:TOK], ALU.mult).then_inc(ss("wide_free"), 1)
                dve.wait_ge(ss("dve_step"), link.n)
                dve.wait_ge(ss("wide_free"), 2 + 24 + c + 1)
                tt(sA[:, 2 * c:2 * c + 2, :], sA[:, 2 * c:2 * c + 2, :], g, ALU.add).then_inc(ss("m_ready"), 1)
                dve.wait_ge(ss("m_hi_ready"), c + 1)
                tt(mT[1][:, 2 * c:2 * c + 2, :], sA[:, 2 * c:2 * c + 2, :], mT[0][:, 2 * c:2 * c + 2, :].bitcast(F), ALU.subtract).then_inc(ss("m_lo_ready"), 1)
            if i in (38, 40):
                blk = (i - 38) // 2
                dve.wait_ge(ss("pe_done"), i)
                for t in range(TILES):
                    rr = rows[0:ROWS[t], t, 512 * blk:512 * blk + 512]
                    stt(out=rr, in0=rr, scalar=ALPHA, in1=ps[0:ROWS[t], triple(blk)[t], :], op0=ALU.mult, op1=ALU.add).then_inc(ss("out_evac"), 1)
            if i == 40:
                dve.wait_ge(ss("out_evac"), 6)
                dve.wait_ge(ss("ln1_in"), 16)
                rows_norm(ln_gb, "h1_rows", tmp=wide)
                for k in range(KT):
                    dve.wait_ge(ss("h1T_hi_s"), k + 1)
                    tt(h1T[1][:, k, :], ps[:, 3 + 4 * (k % 2), 0:TOK], h1T[0][:, k, :].bitcast(F), ALU.subtract).then_inc(ss("h1T_lo_s"), 1)
                route()
            if i in (43, 44):
                gates(i - 43)
        dve.wait_ge(ss("pe_mul"), 6)
        for t in range(TILES):
            q = ROWS[t]
            stt(out=base_rows[0:q, t, :], in0=rows[0:q, t, :], scalar=ALPHA, in1=base_rows[0:q, t, :],
                op0=ALU.mult, op1=ALU.add).then_inc(ss("base_ready"), 1)

        def lo_x(r, e, j):
            dve.wait_ge(ss("hi_ready"), split_of(r, e, j) + 1)
            k = slot_of(e, j)
            tt(lo_slot[k], raw_x[raw_of(e, j)[0]][:], hi_slot[k].bitcast(F), ALU.subtract).then_inc(ss("lo_ready"), 1)

        def x_low(n):
            dve.wait_ge(ss("x_hi"), n + 1)
            tt(xs[:, :, 1, :], ps[:, 0, :].rearrange("p (k s) -> p k s", k=KT), xs[:, :, 0, :].bitcast(F), ALU.subtract).then_inc(ss("x_lo"), 1)

        def act_low(n):
            dve.wait_ge(ss("act_hi"), n + 1)
            tt(aT[:, :, 1, :], ps[:, 3, :].rearrange("p (k s) -> p k s", k=4)[:, :, 0:SLOTS], aT[:, :, 0, :].bitcast(F), ALU.subtract).then_inc(ss("act_lo"), 1)

        def y_sum(n):
            dve.wait_ge(ss("y_copied"), n + 1)
            dve.wait_ge(ss("y_free"), n + 1)
            tt(ysb[:], ps[0:64, 4:6, :].rearrange("p a c -> p (a c)"), ycp[:], ALU.add).then_inc(ss("y_ready"), 1)

        def expert(r, e, first=False, second=False, last=False):
            n = r * EXPERTS + e
            lo_x(r, e, 0)
            lo_x(r, e, 1)
            if first:
                x_low(n)
                pick(r, 1)
                if isinstance(r, int):
                    link(V.memset(act_rows[SLOTS:128, :], 0.0))
            else:
                if not second:
                    y_sum(n - 2)
                act_low(n - 1)
            lo_x(r, e, 3)
            dve.wait_ge(ss("gate_copied"), n + 1)
            tt(gsum[:], ps[0:64, 1, :], gcp[:], ALU.add).then_inc(ss("gate_summed"), 1)
            if not first:
                lo_x(r, e, 4)
            dve.wait_ge(ss("up_copied"), n + 1)
            tt(usum[:], ps[0:64, 2, :], ucp[:], ALU.add).then_inc(ss("up_summed"), 1)
            dve.wait_ge(ss("gate_silued"), n + 1)
            dve.wait_ge(ss("up_summed"), n + 1)
            tt(act_rows[0:SLOTS, :], gsil[:], usum[:], ALU.mult).then_inc(ss("act_ready"), 1)
            if not last:
                x_low(n + 1)
                pick(r, e + 2)

        def rounds(r):
            if not isinstance(r, int):
                ts(iota[:], iota[:], float(SLOTS), None, ALU.add).then_inc(ss("slots_moved"), 1)
                dve.wait_ge(ss("slots_moved"), r)
                pick(r, 0)
            expert(r, 0, first=True)
            expert(r, 1, second=True)
            with dve.Fori(2, EXPERTS - 1) as e:
                expert(r, e)
            expert(r, EXPERTS - 1, last=True)
            lo_x(r, EXPERTS, 0)
            y_sum(r * EXPERTS + EXPERTS - 2)
            act_low(r * EXPERTS + EXPERTS - 1)
            y_sum(r * EXPERTS + EXPERTS - 1)

        rounds(0)
        dve.wait_ge(ss("more_ready"), 1)
        flag = dve.value_load(more[0:1, 0:1], min_val=0, max_val=1)
        with dve.If(flag > 0):
            with dve.Fori(1, ROUNDS) as r:
                rounds(r)

        dve.wait_ge(ss("y_got"), 16 * 6)
        dve.wait_ge(ss("base_ready"), TILES)
        dve.wait_ge(ss("ln2_in"), 16)
        for t in range(TILES):
            q = ROWS[t]
            link(stt(out=base_rows[0:q, t, :], in0=yg[0:q, 0, t, :], scalar=wts[0:q, 0, t:t + 1], in1=base_rows[0:q, t, :],
                     op0=ALU.mult, op1=ALU.add))
            link(stt(out=rows[0:q, t, :], in0=yg[0:q, 1, t, :], scalar=wts[0:q, 1, t:t + 1], in1=base_rows[0:q, t, :],
                     op0=ALU.mult, op1=ALU.add))
        rows_norm(ln_gb, "final_rows", tmp=wide)

    @block.tensor
    def _(pe):
        mm, tr = nc.tensor.matmul, nc.tensor.transpose

        def three(out, wh, wl, xh, xl, first, last):
            mm(out, wh, xh, start=first, stop=False)
            mm(out, wh, xl, start=False, stop=False)
            return mm(out, wl, xh, start=False, stop=last)

        def wide(c, par, src, cols, credit):
            pe.wait_ge(ss("lo_ready"), c + 1)
            pe.wait_ge(ss("wide_free"), credit)
            w = [q[:, par, :].rearrange("p (k c) -> p k c", k=KT) for q in (whi, wlo)]
            for t in range(2):
                out = ps[:, 2 * par + t, 0:cols]
                for k in range(KT):
                    m = three(out, w[0][:, k, 128 * t:128 * t + 128], w[1][:, k, 128 * t:128 * t + 128],
                              src[0][:, k, :], src[1][:, k, :], k == 0, k == KT - 1)
            m.then_inc(ss("pe_done"), 1)

        def row_half(c, par, src, banks, first, last, k0, signal=True):
            pe.wait_ge(ss("lo_ready"), c + 1)
            w = [q[:, par, :].rearrange("p (k c) -> p k c", k=4) for q in (whi, wlo)]
            for t in range(TILES):
                q = ROWS[t]
                out = ps[0:q, banks[t], :]
                for k in range(4):
                    xh, xl = (z[:, k0 + k, 128 * t:128 * t + q] for z in src)
                    mm(out, xh, w[0][:, k, :], start=first and k == 0, stop=False)
                    mm(out, xh, w[1][:, k, :], start=False, stop=False)
                    m = mm(out, xl, w[0][:, k, :], start=False, stop=last and k == 3)
            m.then_inc(ss("pe_done"), 1)

        def transposed(out, src):
            for t in range(TILES):
                q = ROWS[t]
                m = tr(out[:, 128 * t:128 * t + q], src(t), ident[0:q, 0:q])
            return m

        pe.wait_ge(ss("const_in"), 32)
        pe.wait_ge(ss("h_rows"), TILES)
        for k in range(KT):
            if k >= 2:
                pe.wait_ge(ss("hT_lo"), k - 1)
            transposed(ps[:, k % 2, :], lambda t: rows[0:ROWS[t], t, 128 * k:128 * k + 128]).then_inc(ss("hT_psum"), 1)
        pe.wait_ge(ss("hT_lo"), KT)
        with pe.Fori(0, 4) as n:
            for par in range(2):
                wide(n * 2 + par, par, hT, TOK, n * 2 + (par + 1))
        with pe.Fori(0, 2) as n:
            for b in range(2):
                pe.wait_ge(ss("row_free"), n * 6 + (3 * b + 3))
                if b == 1:
                    pe.wait_ge(ss("wide_free"), 2 + 8)
                for half in range(2):
                    row_half(n * 4 + (QKV0 + 2 * b + half), half, hT, triple(b), half == 0, half == 1, 4 * half)

        def heads_T(h):
            for w in range(2):
                m = transposed(ps[:, 2 * (h % 2) + w, :], lambda t: qk[0:ROWS[t], w, t, h * DK:(h + 1) * DK])
            m.then_inc(ss("heads_T"), 1)

        pe.wait_ge(ss("v_ready"), 2 * TILES)
        pe.wait_ge(ss("qk_rows"), 4 * TILES)
        pe.wait_ge(ss("state_in"), 16)
        heads_T(0)
        for h in range(HEADS):
            if h + 1 < HEADS:
                heads_T(h + 1)
            pe.wait_ge(ss("heads_copied"), 2 * (h + 1))
            if h >= 1:
                pe.wait_ge(ss("masked"), 3 * h)
            qT, kT = qkT[:, h % 2, 0, :], qkT[:, h % 2, 1, :]
            mm(ps[:, 4, 0:256], kT[:, 0:128], qT[:, 0:256], start=True, stop=True)
            mm(ps[:, 4, 256:384], kT[:, 128:256], qT[:, 128:256], start=True, stop=True)
            mm(ps[0:64, 4, 384:448], kT[:, 256:320], qT[:, 256:320], start=True, stop=True).then_inc(ss("scores"), 1)
            pe.wait_ge(ss("kz_ready"), 3 * (h + 1))
            if h >= 1:
                pe.wait_ge(ss("kv_out"), 2 * h)
            v = [vrow[0:ROWS[t], t, h * DV:(h + 1) * DV] for t in range(TILES)]
            kz = [qk[0:ROWS[t], 1, t, h * DK:(h + 1) * DK] for t in range(TILES)]
            mm(ps[:, 7, 0:DV], kz[0], v[0], start=True, stop=False)
            mm(ps[:, 7, 0:DV], kz[1], v[1], start=False, stop=True)
            mm(ps[:, 7, DV:2 * DV], kz[2], v[2], start=True, stop=True).then_inc(ss("kv_ready"), 1)
            pe.wait_ge(ss("masked"), 3 * (h + 1))
            if h >= 1:
                pe.wait_ge(ss("on_ready"), 3 * h)
            sc = sT[:, h % 2, :]
            mm(ps[:, 5, 0:DV], sc[:, 0:128], v[0], start=True, stop=True)
            mm(ps[:, 5, DV:2 * DV], sc[:, 128:256], v[0], start=True, stop=False)
            mm(ps[:, 5, DV:2 * DV], sc[:, 256:384], v[1], start=False, stop=True)
            mm(ps[0:64, 6, 0:DV], sT[0:64, h % 2, 384:448], v[2], start=True, stop=False)
            mm(ps[0:64, 6, 0:DV], qx[:, h % 2, :], rstate[:, h, :], start=False, stop=True).then_inc(ss("o_ready"), 1)
        with pe.Fori(0, 2) as n:
            for par in range(2):
                wide(n * 2 + (G0 + par), par, hT, TOK, n * 2 + (8 + par + 1))
        pe.wait_ge(ss("on_ready"), 3 * HEADS)
        for v in range(KT):
            if v >= 2:
                pe.wait_ge(ss("at_ready"), v - 1)
            transposed(ps[:, 5 + v % 2, :], lambda t: on[0:ROWS[t], t, 128 * v:128 * v + 128]).then_inc(ss("onT_psum"), 1)
        with pe.Fori(0, 2) as n:
            for par in range(2):
                wide(n * 2 + (GA0 + par), par, hT, TOK, n * 2 + (12 + par + 1))
        pe.wait_ge(ss("at_lo"), KT)
        with pe.Fori(0, 2) as n:
            for par in range(2):
                wide(n * 2 + (RET0 + par), par, AT, TOK, n * 2 + (16 + par + 1))
        wide(GB0, 0, hT, TOK, 21)
        pe.wait_ge(ss("taps_done"), KT * CONV_W)
        for j in range(KT):
            m = mm(ps[:, 7, 0:CCOLS], meanw, cT[:, j, :], start=j == 0, stop=j == KT - 1)
        m.then_inc(ss("mean_ready"), 1)
        wide(GB0 + 1, 1, hT, TOK, 22)
        pe.wait_ge(ss("squared"), 1)
        for j in range(KT):
            m = mm(ps[:, 7, 0:CCOLS], meanw, sq[:, j, :], start=j == 0, stop=j == KT - 1)
        m.then_inc(ss("var_ready"), 1)
        wide(GB0 + 2, 0, hT, TOK, 23)
        wide(GB0 + 3, 1, hT, TOK, 24)
        pe.wait_ge(ss("ct_lo"), KT)
        with pe.Fori(0, 2) as n:
            for par in range(2):
                wide(n * 2 + (CONV0 + par), par, CT, CCOLS, n * 2 + (24 + par + 1))
        pe.wait_ge(ss("m_lo_ready"), 4)
        for b in range(2):
            if b == 1:
                pe.wait_ge(ss("wide_free"), 2 + 28)
            for half in range(2):
                row_half(OUT0 + 2 * b + half, half, mT, triple(b), half == 0, half == 1, 4 * half)
        pe.wait_ge(ss("h1_rows"), TILES)
        for k in range(KT):
            if k >= 2:
                pe.wait_ge(ss("h1T_lo_s"), k - 1)
            transposed(ps[:, 3 + 4 * (k % 2), :], lambda t: rows[0:ROWS[t], t, 128 * k:128 * k + 128]).then_inc(ss("h1T_psum"), 1)
        pe.wait_ge(ss("h1T_copied"), KT)
        pe.wait_ge(ss("h1T_lo_s"), KT)
        pe.wait_ge(ss("route_in"), 32)
        for k in range(KT):
            m = mm(ps[0:36, 3, 0:TOK], w_route[:, k, :], h1T_f[:, k, :], start=k == 0, stop=k == KT - 1)
        m.then_inc(ss("logT_psum"), 1)
        pe.wait_ge(ss("logT_ready"), 1)
        for t in range(TILES):
            m = tr(ps[0:ROWS[t], 7, 36 * t:36 * t + 36], logT[:, 128 * t:128 * t + ROWS[t]], ident[0:36, 0:36])
        m.then_inc(ss("logit_psum"), 1)
        pe.wait_ge(ss("taken_ready"), 1)
        for t in range(TILES + 1):
            n = min(t, TILES - 1)
            for f in range(n + 1):
                m = mm(ps[:, 7, 128 + 32 * t:160 + 32 * t], triu[:, 0 if t == f else 1, :], taken16[:, f, :],
                       start=f == 0, stop=f == n)
        m.then_inc(ss("rank_psum"), 1)

        def gather(r, e):
            pe.wait_ge(ss("onehot_ready"), r * (EXPERTS + 1) + e + 1)
            for k in range(KT):
                for part in range(3):
                    for t in range(TILES):
                        m = mm(ps[:, 0, SLOTS * k:SLOTS * k + SLOTS], h1b[:, part, t, 128 * k:128 * k + 128], onehot[:, t, :],
                               start=part == 0 and t == 0, stop=part == 2 and t == TILES - 1)
            m.then_inc(ss("x_gathered"), 1)

        pe.wait_ge(ss("lo_ready"), PROJ0 + 1)
        pe.wait_ge(ss("pT_lo_s"), 1)
        pe.wait_ge(ss("out_evac"), 6)
        w = [q[:, PROJ0 % 2, :].rearrange("p (k c) -> p k c", k=2) for q in (whi, wlo)]
        for b in range(2):
            for t in range(TILES):
                q = ROWS[t]
                for k in range(2):
                    xh, xl = (z[:, k, 128 * t:128 * t + q] for z in pT)
                    out = ps[0:q, triple(b)[t], :]
                    mm(out, xh, w[0][:, k, 512 * b:512 * b + 512], start=k == 0, stop=False)
                    mm(out, xh, w[1][:, k, 512 * b:512 * b + 512], start=False, stop=False)
                    m = mm(out, xl, w[0][:, k, 512 * b:512 * b + 512], start=False, stop=k == 1)
        m.then_inc(ss("pe_done"), 1)
        for b in range(2):
            pe.wait_ge(ss("proj_evac"), 3 * b + 3)
            for half in range(2):
                row_half(GATE0 + 2 * b + half, (GATE0 + half) % 2, h1T, triple(b), half == 0, half == 1, 4 * half)
        pe.wait_ge(ss("part_last"), 1)
        pe.wait_ge(ss("gate_sig_s"), 6)
        gather(0, 0)

        def product(r, e, j, stat, banks, k0, kts, first, last, whole=False):
            slot, fills = raw_of(e, j)
            if whole:
                pe.wait_ge(raw_x_in[slot], (fills + EXPERTS * r) * 16 + 16)
                parts = (raw_x[slot][:],)
            else:
                pe.wait_ge(ss("lo_ready"), split_of(r, e, j) + 1)
                parts = (hi_slot[slot_of(e, j)], lo_slot[slot_of(e, j)])
            for k in range(kts):
                rows_k = stat[:, k0 + k, :, :].rearrange("p a s -> p (a s)")
                for b in range(len(banks)):
                    for n, q in enumerate(parts):
                        wv = q.rearrange("p (k c) -> p k c", k=kts)
                        m = mm(ps[:, banks[b], :], rows_k.bitcast(F) if whole else rows_k, wv[:, k, 512 * b:512 * b + 512],
                               start=first and k == 0 and n == 0, stop=last and k == kts - 1 and n == len(parts) - 1)
            m.then_inc(ss("pe_done"), 1)

        def down(r, e, j0):
            pe.wait_ge(ss("act_lo"), r * EXPERTS + e)
            if not (isinstance(e, int) and e == 1):
                pe.wait_ge(ss("y_ready"), r * EXPERTS + e - 1)
            product(r, e, j0, aT, (4, 5), 0, 2, True, False)
            product(r, e, j0 + 1, aT, (4, 5), 2, 2, False, True, whole=True)

        def expert(r, e, first=False, last=False):
            n = r * EXPERTS + e
            pe.wait_ge(ss("x_lo"), n + 1)
            product(r, e, 0, xs, (1,), 0, 4, True, False)
            product(r, e, 1, xs, (1,), 4, 4, False, True)
            product(r, e, 2, xs, (2,), 0, 4, True, False, whole=True)
            if not last:
                gather(r, e + 1)
            product(r, e, 3, xs, (2,), 4, 4, False, True)
            if not first:
                down(r, e, 4)
            pe.wait_ge(ss("act_ready"), n + 1)
            for f in range(FF // 128):
                m = tr(ps[:, 3, 128 * f:128 * f + 128], act_rows[:, 128 * f:128 * f + 128], ident)
            m.then_inc(ss("act_T"), 1)

        def rounds(r):
            if not isinstance(r, int):
                gather(r, 0)
            expert(r, 0, first=True)
            with pe.Fori(1, EXPERTS - 1) as e:
                expert(r, e)
            expert(r, EXPERTS - 1, last=True)
            down(r, EXPERTS, 0)

        rounds(0)
        pe.wait_ge(ss("more_ready"), 1)
        flag = pe.value_load(more[0:1, 0:1], min_val=0, max_val=1)
        with pe.If(flag > 0):
            with pe.Fori(1, ROUNDS) as r:
                rounds(r)

    block.__exit__(None, None, None)


def _wide(w, c):
    return w[:, 256 * c:256 * c + 256].reshape(KT, 128, 256).transpose(1, 0, 2).reshape(128, CH)


def _part(w, b, half):
    return w[512 * half:512 * half + 512, 512 * b:512 * b + 512].reshape(4, 128, 512).transpose(1, 0, 2).reshape(128, CH)


def _two_rows(w):
    return w.reshape(2, 128, 1024).transpose(1, 0, 2).reshape(128, CH)


def _stream(w_in, w_ret, w_conv, w_out, w_proj, w_gate, eg, eu, ed):
    out = np.empty((DENSE + PER_ROUND, 128, CH), w_in.dtype)
    a, b = w_in[:, 3072:4096], w_in[:, 4096:5120]
    for j in range(KT):
        pair = np.concatenate([a[:, 128 * j:128 * j + 128], b[:, 128 * j:128 * j + 128]], axis=1)
        out[GLU0 + j] = _wide(pair, 0)
    for blk in range(4):
        for half in range(2):
            out[QKV0 + 2 * blk + half] = _part(w_in[:, 0:2048], blk, half)
    for first, w in ((G0, w_in[:, 2048:3072]), (GA0, w_in[:, 5120:6144]), (RET0, w_ret), (GB0, w_in[:, 6144:7168]), (CONV0, w_conv)):
        for c in range(4):
            out[first + c] = _wide(w, c)
    for first, w in ((OUT0, w_out), (GATE0, w_gate)):
        for blk in range(2):
            for half in range(2):
                out[first + 2 * blk + half] = _part(w, blk, half)
    out[PROJ0] = _two_rows(w_proj)
    i = DENSE
    for e in range(EXPERTS + 1):
        if e < EXPERTS:
            for w in (eg[e], eu[e]):
                for half in range(2):
                    out[i] = _part(w, 0, half)
                    i += 1
        if e > 0:
            for half in range(2):
                out[i] = _two_rows(ed[e - 1][256 * half:256 * half + 256])
                i += 1
    return out


_OUTS = [("y", (TOK, D_MODEL)), ("ret_p", (HEADS, DK, DV)), ("ret_s", (HEADS, DK, DV)),
         ("conv_p", (128, KT, HIST)), ("conv_s", (128, KT, HIST))]


def kernel(**inputs):
    import ml_dtypes
    from concourse import bacc
    from concourse.bass_utils import run_bass_kernel_spmd

    i = {k: np.asarray(v) for k, v in inputs.items()}

    def by_channel(v):
        return np.moveaxis(v.reshape(*v.shape[:-1], KT, 128), (-1, -2), (0, 1))

    flat = lambda w: w.reshape(EXPERTS, *w.shape[-2:])
    t = np.arange(128)
    arrays = {
        "wstream": _stream(i["w_in"][0], i["w_ret_out"][0], i["w_conv_out"][0], i["w_out"][0], i["w_ple_proj"][0],
                           i["w_ple_gate"][0], flat(i["w_exp_gate"]), flat(i["w_exp_up"]), flat(i["w_exp_down"])),
        "x": np.concatenate([i["x_prompt"][0], i["x_sample"][0]]),
        "p_t": np.concatenate([i["p_prompt"][0, 0], i["p_sample"][0, 0]]).T.reshape(2, 128, TOK).transpose(1, 0, 2),
        "state_ret": i["state_ret"][0, 0],
        "state_conv": by_channel(i["state_conv"][0, 0]),
        "consts": _constants(),
        "triangle": np.stack([t[:, None] < t[None, :], np.ones((128, 128), bool)], axis=1).astype(ml_dtypes.bfloat16),
        "conv_params": np.concatenate([by_channel(i[n][0].reshape(-1, D_MODEL)) for n in ("conv_w", "conv_b", "conv_ln_g", "conv_ln_b")], axis=2),
        "route_w": np.concatenate([i["w_route_g"][0], *i["w_route_e"][0]], axis=1).reshape(KT, 128, 36).transpose(1, 0, 2),
        "route_b": np.concatenate([i["b_route_g"][0], i["b_route_e"][0].ravel()])[:, None],
        "ln_in": np.stack([i["ln_in_g"], i["ln_in_b"]]),
        "ln1": np.stack([i["ln1_g"][0], i["ln1_b"][0]]),
        "ln2": np.stack([i["ln2_g"][0], i["ln2_b"][0]]),
    }
    arrays = {k: np.ascontiguousarray(v) for k, v in arrays.items()}
    nc = bacc.Bacc("TRN2", target_bir_lowering=False, num_devices=1)
    args = [nc.dram_tensor(k, list(v.shape), mybir.dt.from_np(v.dtype), kind="ExternalInput").ap() for k, v in arrays.items()]
    args += [nc.dram_tensor(k, list(shape), mybir.dt.float32, kind="ExternalOutput").ap() for k, shape in _OUTS]
    _program(nc, *args)
    r = run_bass_kernel_spmd(nc, [arrays], core_ids=[0]).results[0]

    def history(v):
        return np.ascontiguousarray(np.asarray(v).transpose(2, 1, 0).reshape(1, 1, HIST, D_MODEL))

    yy = np.asarray(r["y"])
    return (yy[None, :SEQ], yy[None, SEQ:], np.asarray(r["ret_p"])[None, None], history(r["conv_p"]),
            np.asarray(r["ret_s"])[None, None], history(r["conv_s"]))
```

```python
import math

import numpy as np

import concourse.bass as bass
from concourse import mybir

D_MODEL, SEQ, DEC_SEQ, PAST_LEN, CHUNK = 1024, 256, 64, 512, 64
TOK = SEQ + DEC_SEQ
TILES = 3
ROWS = [128, 128, 64]
KT = D_MODEL // 128
HEADS, DK, DV = 4, 128, 256
CONV_W = 31
HIST = CONV_W - 1
UCOLS = HIST + SEQ + HIST + DEC_SEQ
CCOLS = UCOLS - HIST
S0 = SEQ + HIST
GROUPS, PER_GROUP = 4, 8
EXPERTS = GROUPS * PER_GROUP
FF = 512
PLE = 256
EPS = 1e-5
ALPHA = 2.0 ** 0.25
SLOTS = 64
ROUNDS = -(-TOK // SLOTS)
BIG = 1e30

CH = 2048
GLU0, QKV0, G0, GA0, RET0, GB0, PROJ0, CONV0, OUT0, GATE0, DENSE = 0, 8, 16, 20, 24, 28, 32, 33, 37, 41, 45
PER_ROUND = 6 * EXPERTS
SPLIT = {0: 0, 1: 1, 3: 2, 4: 3}
RAW_D, RAW_X = 4, 6

C_ID, C_ONES, C_MASK = 0, 128, 256
C_XI = C_MASK + HEADS * 448
C_ZETA = C_XI + HEADS * 64
C_COS = C_ZETA + 12
C_SIN = C_COS + 192
C_IOTA = C_SIN + 192
C_EOFF = C_IOTA + 64
C_PRIO4 = C_EOFF + EXPERTS
C_PRIO8 = C_PRIO4 + 4
C_FOLD = C_PRIO8 + 8
C_N = C_FOLD + 36
TAP_GROUPS = ((1, 2), (3, 4), (5, 6, 7))
WARM = (16, 6, 9, 3, 5, 6, 5, 3, 15, 5)
GAMMA = [1.0 - 2.0 ** (-5.0 - h) for h in range(HEADS)]


def _constants():
    c = np.zeros((128, C_N), np.float64)
    p = np.arange(128)
    c[:, C_ID:C_ID + 128] = np.eye(128)
    c[:, C_ONES:C_ONES + 128] = 1.0 / D_MODEL
    scale = DK ** -0.5
    for h, g in enumerate(GAMMA):
        m = C_MASK + 448 * h
        for first, cols in ((0, np.arange(256)), (128, np.arange(128, 256))):
            src, dst = (first + p)[:, None], cols[None, :]
            seen = (dst >= src) | (dst // CHUNK == src // CHUNK)
            c[:, m + 2 * first:m + 2 * first + len(cols)] = np.where(seen, g ** np.abs(dst - src), 0.0) * scale
        l = np.arange(64)
        c[:64, m + 384:m + 448] = g ** np.abs(l[None, :] - l[:, None]) * scale
        c[:, C_XI + 64 * h:C_XI + 64 * (h + 1)] = g ** (l + 1.0)
        for t in range(TILES):
            last = 255 - 128 * t - p if t < 2 else np.maximum(63 - p, 0)
            c[:, C_ZETA + 4 * t + h] = g ** last * scale
    half = DK // 2
    inv = np.float32(10000.0) ** (-np.arange(half, dtype=np.float32) / np.float32(half))
    for t in range(TILES):
        pos = (128 * t + p if t < 2 else PAST_LEN + p % 64).astype(np.float32)
        ang = pos[:, None] * inv[None, :]
        c[:, C_COS + 64 * t:C_COS + 64 * (t + 1)] = np.cos(ang)
        c[:, C_SIN + 64 * t:C_SIN + 64 * (t + 1)] = np.sin(ang)
    c[:, C_IOTA:C_IOTA + 64] = np.arange(64)
    c[:, C_EOFF:C_EOFF + EXPERTS] = SLOTS * np.arange(EXPERTS)
    c[:, C_PRIO4:C_PRIO4 + 4] = 4 - np.arange(4)
    c[:, C_PRIO8:C_PRIO8 + 8] = 8 - np.arange(8)
    c[:72, C_FOLD:C_FOLD + 36] = np.concatenate([np.eye(36), np.eye(36)])
    return c.astype(np.float32)


class Area:

    def __init__(self, nc, start, size):
        self.nc, self.start, self.next, self.end = nc, start, start, start + size

    def put(self, name, shape, dt, width=4):
        size = -(-int(np.prod(shape[1:])) * width // 32) * 32
        assert self.next + size <= self.end, (name, self.next + size - self.end)
        self.next += size
        return self.nc.alloc_sbuf_tensor_at(name, list(shape), dt, offset=self.next - size)


class Chain:

    def __init__(self, engine, sem):
        self.engine, self.sem, self.n = engine, sem, 0

    def __call__(self, instruction):
        self.n += 1
        instruction.then_inc(self.sem, 1)
        self.engine.wait_ge(self.sem, self.n)


def _program(nc, wstream, x, p_t, state_ret, state_conv, consts, triangle, conv_params, route_w, route_b,
             ln_in, ln1, ln2, y, ret_p, ret_s, conv_p, conv_s):
    F, R, B16 = mybir.dt.float32, mybir.dt.float32r, mybir.dt.bfloat16
    U32, I32 = mybir.dt.uint32, mybir.dt.int32
    ALU, ACT, X = mybir.AluOpType, mybir.ActivationFunctionType, mybir.AxisListType.X
    ds = bass.ds

    y_rows = nc.dram_tensor("y_rows", [ROUNDS * EXPERTS * SLOTS, D_MODEL], F, kind="Internal").ap()

    begin, end = -(-nc.sbuf_base // 32) * 32, nc.sbuf_usable_end // 32 * 32
    sizes = dict(fixed=15328, rows=12288, ring=RAW_D * CH * 4, split=4 * CH * 4, h=20480, u=12160, c=11200,
                 qk=21504, v=24576, g=10240, ga=10240)
    o, spot = begin, {}
    for name, size in sizes.items():
        spot[name] = o
        o += size
    spot["ret"] = o

    def area(name, size=None, skip=0):
        return Area(nc, spot[name] + skip, size if size else sizes[name] - skip)

    a = area("fixed")
    const = a.put("const", [128, C_N], F)
    triu = a.put("triu", [128, 2, 128], B16, 2)
    conv_par = a.put("conv_par", [128, KT, CONV_W + 3], F)
    w_route = a.put("w_route_sb", [128, KT, 36], F)
    b_route = a.put("b_route_sb", [72, 1], F)
    stats = a.put("stats", [128, 6, 6], F)
    mv = a.put("mv", [128, TILES, 2], F)
    rstd = a.put("rstd", [128, TILES], F)
    rows = area("rows").put("rows_sb", [128, TILES, D_MODEL], F)
    raw_d = area("ring").put("raw_dense", [128, RAW_D, CH], F)
    a = area("split")
    whi = a.put("w_hi", [128, 2, CH], R)
    wlo = a.put("w_lo", [128, 2, CH], R)
    a = area("h")
    hT = [a.put("hT_hi", [128, KT, TOK], R), a.put("hT_lo", [128, KT, TOK], R)]
    uT = area("u").put("uT_sb", [128, KT, UCOLS], F)
    cT = area("c").put("cT_sb", [128, KT, CCOLS], F)
    a = area("qk")
    qk = a.put("qk_rows", [128, 2, TILES, 512], F)
    qkT = a.put("qkT", [128, 2, 2, TOK], F)
    rot = a.put("rot", [128, 2, 512], F)
    a = area("v")
    vrow = a.put("v_rows", [128, TILES, D_MODEL], F)
    on = a.put("on_rows", [128, TILES, D_MODEL], F)
    tap_a = area("ga").put("tap_diag_a", [128, 20, 128], F)
    tap_b = Area(nc, spot["v"] + 12288, 12288).put("tap_diag_b", [128, CONV_W - 20, 128], F)
    tap_diag = [tap_a[:, k, :] if k < 20 else tap_b[:, k - 20, :] for k in range(CONV_W)]
    gT = area("g").put("gT", [128, KT, TOK], F)
    sA = area("ga").put("sA", [128, KT, TOK], F)
    a = area("ret", end - spot["ret"])
    rstate = a.put("rstate", [128, HEADS, DV], F)
    sT = a.put("sT", [128, 2, 448], F)
    qx = a.put("qx", [128, 2, 64], F)
    kv_s = a.put("kv_sample", [128, DV], F)
    ln_in_gb = area("ga").put("ln_in_gb", [128, 2, D_MODEL], F)
    a = area("g")
    glu_sig = a.put("glu_sig", [128, 2, TOK], F)
    ln_tmp = a.put("ln_tmp", [128, D_MODEL], F)
    ret_out = Area(nc, spot["qk"] + 12288 + 5120, 4096).put("ret_out", [128, HEADS, DV], F)
    sB = area("g").put("sB", [128, KT, TOK], F)
    a = area("qk")
    AT = [a.put("AT_hi", [128, KT, TOK], R), a.put("AT_lo", [128, KT, TOK], R)]
    a = area("v")
    CT = [a.put("CT_hi", [128, KT, CCOLS], R), a.put("CT_lo", [128, KT, CCOLS], R)]
    sq = area("u").put("sq", [128, KT, CCOLS], F)
    a = area("h")
    mT = [a.put("m_hi", [128, KT, TOK], R), a.put("m_lo", [128, KT, TOK], R)]
    a = area("ret", end - spot["ret"])
    cstat = a.put("cstat", [128, CCOLS], F)
    at_tmp = Area(nc, spot["ret"] + 4096, 3584).put("at_tmp", [128, 2, TOK], F)
    a = area("h")
    h1T = [a.put("h1T_hi", [128, KT, TOK], R), a.put("h1T_lo", [128, KT, TOK], R)]
    raw_x = [Area(nc, s, CH * 4).put(f"raw_x{i}", [128, CH], F) for i, s in enumerate(
        (spot["u"], spot["u"] + CH * 4, spot["v"], spot["v"] + CH * 4, spot["v"] + 2 * CH * 4, spot["g"]))]
    a = Area(nc, spot["u"] + 2 * CH * 4, spot["v"] - spot["u"] - 2 * CH * 4)
    ln_gb = a.put("ln_gb", [128, 2, D_MODEL], F)
    pT_at = a.next
    pT_raw = a.put("pT_raw", [128, 2, TOK], F)
    pT = [a.put("pT_hi", [128, 2, TOK], R), a.put("pT_lo", [128, 2, TOK], R)]
    base_rows = a.put("base_rows", [128, TILES, D_MODEL], F)
    a = area("ga", end - spot["ga"])
    h1b = a.put("h1b", [128, 3, TILES, D_MODEL], B16, 2)
    rankm = a.put("rankm", [128, TILES, EXPERTS + 1], F)
    iota = a.put("iota_r", [128, SLOTS], F)
    wts = a.put("wts", [128, 2, TILES], F)
    pos_u = a.put("pos_u", [128, 2, TILES], U32)
    more = a.put("more", [1, 1], I32)
    a = area("g", skip=CH * 4)
    logT = a.put("logT", [72, TOK], F)
    onehot = a.put("onehot", [128, TILES, SLOTS], B16, 2)
    a = area("fixed", 4 * (C_IOTA - C_MASK), skip=4 * C_MASK)
    w_route_r = a.put("w_route_parts", [128, KT, 2, 36], R)
    logit = a.put("logit", [128, TILES, 36], F)
    r4 = a.put("r4", [128, TILES, 4], F)
    gsel = a.put("gsel", [128, TILES, 4], F)
    e32 = a.put("e32", [128, TILES, EXPERTS], F)
    e8 = a.put("e8", [128, 2, TILES, 8], F)
    s8 = a.put("s8", [128, 2, TILES, 8], F)
    r1 = a.put("r1", [128, 12, TILES], F)
    sel = a.put("sel", [128, 2, TILES, EXPERTS], F)
    taken = a.put("taken", [128, TILES, EXPERTS], F)
    taken16 = a.put("taken16", [128, TILES, EXPERTS], B16, 2)
    rank = a.put("rank", [128, TILES + 1, EXPERTS], F)
    wide = a.put("wide_tmp", [128, D_MODEL], F)
    gate_sig = Area(nc, pT_at, 7680).put("gate_sig", [128, 2, 512], F)
    a = area("ring")
    whi_x = [a.put(f"w_hi_x{i}", [128, CH], R) for i in range(2)]
    wlo_x = [a.put(f"w_lo_x{i}", [128, CH], R) for i in range(2)]
    hi_slot = [whi_x[0][:], whi_x[1][:], whi[:, 1, :], whi[:, 0, :]]
    lo_slot = [wlo_x[0][:], wlo_x[1][:], wlo[:, 1, :], wlo[:, 0, :]]
    a = area("h")
    xs = a.put("xs", [128, KT, 2, SLOTS], R)
    gcp = a.put("gate_cp", [64, FF], F)
    gsum = a.put("gate_sum", [64, FF], F)
    gsil = a.put("gate_silu", [64, FF], F)
    usum = a.put("up_sum", [64, FF], F)
    act_rows = a.put("act_rows", [128, FF], F)
    aT = a.put("actT", [128, FF // 128, 2, SLOTS], R)
    ycp = a.put("y_cp", [64, D_MODEL], F)
    a = Area(nc, pT_at, 7680)
    ucp = a.put("up_cp", [64, FF], F)
    ysb = a.put("y_sb", [64, D_MODEL], F)
    wdiag = Area(nc, spot["ring"], 4096).put("weight_diag", [128, TILES, 2, 128], F)
    yg = area("split").put("y_gathered", [128, 2, TILES, D_MODEL], F)

    ps = nc.alloc_psum_tensor("ps", [128, 8, 512], F)
    ident = const[:, C_ID:C_ID + 128]
    meanw = const[:, C_ONES:C_ONES + 128]

    s = {n: nc.alloc_semaphore(n) for n in (
        "ident_in const_in ln_in_in conv_in state_in route_in ln1_in ple_in ln2_in "
        "h_rows hT_psum hT_hi hT_lo hi_ready lo_ready pe_done wide_free row_free sig_ready v_ready qk_rows "
        "heads_T heads_copied kz_ready q_scaled scores masked kv_ready kv_out state_new o_ready on_ready "
        "diag_ready conv0_psum conv0_ready states_out ret_p_out out_tile route_hi route_lo "
        "onT_psum at_ready at_hi at_lo taps_done mean_ready centred squared var_ready cstd_ready conv_norm "
        "silu_ready ct_hi ct_lo m_ready m_hi_ready m_lo_ready out_evac "
        "var_in root_out h1_rows h1T_psum h1T_hi_s h1T_lo_s pT_hi_s pT_lo_s part_hi part_rest part_mid part_last "
        "logT_psum logT_ready logit_psum gexp_in gexp eexp_in eexp taken_ready rank_psum "
        "proj_psum proj_evac gate_sig_s pe_mul base_ready conv_out1 "
        "onehot_ready x_gathered x_hi x_lo gate_copied gate_summed gate_silued up_copied up_summed act_ready "
        "act_T act_hi act_lo y_copied y_ready y_stored y_free slots_moved pos_ready more_ready "
        "wdiag_ready sum_psum final_rows y_out "
        "dve_step").split()}
    x_in = [nc.alloc_semaphore(f"x_in{t}") for t in range(TILES)]
    y_got = [nc.alloc_semaphore(f"y_got{t}") for t in range(TILES)]
    raw_d_in = [nc.alloc_semaphore(f"raw_dense_in{i}") for i in range(RAW_D)]
    raw_x_in = [nc.alloc_semaphore(f"raw_expert_in{i}") for i in range(RAW_X)]

    def ss(name):
        return s[name]

    def triple(b):
        return (4, 5, 6) if b % 2 == 0 else (0, 1, 2)

    PROJ_BANKS = ((4, 5, 6), (7, 0, 1))
    GATE_BANKS = ((4, 5, 6), (0, 3, 2))

    CT_PARTS = (range(2), range(2, 5), range(5, KT))

    def chunk_of(r, e, j):
        return DENSE + r * PER_ROUND + (j if isinstance(e, int) and e == 0 else 4 + (e - 1) * 6 + j)

    def sum_psum(t):
        b = (0, 2, 6)[t]
        return ps[0:ROWS[t], b:b + 2, :].rearrange("p b c -> p (b c)")

    def rowsT_psum(t):
        if ROWS[t] == 64:
            return ps[:, 0, :].rearrange("p (k c) -> p k c", k=KT)
        return ps[:, 4 + 2 * t:6 + 2 * t, :].rearrange("p b (k c) -> p (b k) c", k=KT // 2)

    def split_of(r, e, j):
        return DENSE + r * 4 * EXPERTS + (SPLIT[j] if isinstance(e, int) and e == 0 else 3 + (e - 1) * 4 + SPLIT[j])

    def slot_of(e, j):
        return SPLIT[j] if isinstance(e, int) and e == 0 else (3 + SPLIT[j]) % 4

    def raw_of(e, j):
        if isinstance(e, int) and e == 0:
            return j, 0
        return (4 + j) % 6, (e - 1 if j < 2 else e)

    def round_start(r):
        return DENSE + r * PER_ROUND

    block = nc.Block()
    block.__enter__()

    @block.sync
    def _(sp):
        for t in range(TILES):
            sp.dma_start(rows[0:ROWS[t], t, :], x[128 * t:128 * t + ROWS[t], :]).then_inc(x_in[t], 16)
            if t == 1:
                sp.dma_start(ln_in_gb[:], ln_in.unsqueeze(0).broadcast_to([128, 2, D_MODEL])).then_inc(ss("ln_in_in"), 16)
        sp.dma_start(const[:, 0:C_MASK], consts[:, 0:C_MASK]).then_inc(ss("ident_in"), 16)
        for i in range(RAW_D):
            sp.dma_start(raw_d[:, i, :], wstream[i]).then_inc(raw_d_in[i], 16)
            if i == 1:
                sp.dma_start(const[:, C_MASK:], consts[:, C_MASK:]).then_inc(ss("const_in"), 16)
                sp.dma_start(triu[:], triangle).then_inc(ss("const_in"), 16)
        with sp.Fori(1, 11) as n:
            for i in range(RAW_D):
                sp.wait_ge(ss("lo_ready"), n * RAW_D + (i - RAW_D + 1))
                sp.dma_start(raw_d[:, i, :], wstream[ds(n * RAW_D + i, 1)].rearrange("a p c -> (a p) c")).then_inc(raw_d_in[i], 16)
        sp.wait_ge(ss("m_ready"), 4)
        for l in range(4):
            sp.dma_start(raw_x[l][:], wstream[DENSE + l]).then_inc(raw_x_in[l], 16)
        for l in range(4, RAW_X):
            sp.dma_start(raw_x[l][:], wstream[DENSE + l]).then_inc(raw_x_in[l], 16)
        sp.wait_ge(ss("lo_ready"), DENSE - RAW_D)
        sp.dma_start(raw_d[:, 0, :], wstream[DENSE - 1]).then_inc(raw_d_in[0], 16)

        def fetch(r, e, j):
            slot = raw_of(e, j)[0]
            sp.dma_start(raw_x[slot][:], wstream[ds(chunk_of(0, e, j), 1)].rearrange("a p c -> (a p) c")).then_inc(raw_x_in[slot], 16)

        def fetch_round(r):
            if not (isinstance(r, int) and r == 0):
                sp.wait_ge(ss("pe_done"), round_start(r))
                for j in range(4):
                    fetch(r, 0, j)
                for j in range(2):
                    fetch(r, 1, j)
            for j in range(2, 6):
                if j - 2 in SPLIT:
                    sp.wait_ge(ss("lo_ready"), split_of(r, 0, j - 2) + 1)
                else:
                    sp.wait_ge(ss("pe_done"), chunk_of(r, 0, j - 2) + 1)
                fetch(r, 1, j)

            def after_same(e, j):
                if j in SPLIT:
                    sp.wait_ge(ss("lo_ready"), split_of(r, e, j) - 3)
                else:
                    sp.wait_ge(ss("pe_done"), chunk_of(r, e, j) - 5)
                fetch(r, e, j)

            with sp.Fori(2, EXPERTS) as e:
                for j in range(6):
                    after_same(e, j)
            for j in range(2):
                after_same(EXPERTS, j)

        fetch_round(0)
        sp.wait_ge(ss("more_ready"), 1)
        flag = sp.value_load(more[0:1, 0:1], min_val=0, max_val=1)
        with sp.If(flag > 0):
            with sp.Fori(1, ROUNDS) as r:
                fetch_round(r)
        for t in range(TILES):
            sp.wait_ge(ss("final_rows"), t + 1)
            sp.dma_start(y[128 * t:128 * t + ROWS[t], :], rows[0:ROWS[t], t, :]).then_inc(ss("y_out"), 16)
        sp.wait_ge(ss("y_out"), 16 * TILES)

    @block.gpsimd
    def _(pool):
        pool.dma_start(conv_par[:], conv_params).then_inc(ss("conv_in"), 16)
        pool.dma_start(uT[:, :, S0:S0 + HIST], state_conv).then_inc(ss("conv_in"), 16)
        pool.wait_ge(ss("h_rows"), TILES)
        pool.dma_start(rstate[:], state_ret.rearrange("h p c -> p h c")).then_inc(ss("state_in"), 16)
        pool.dma_start(w_route[:], route_w).then_inc(ss("route_in"), 16)
        pool.dma_start(b_route[:], route_b).then_inc(ss("route_in"), 16)
        pool.wait_ge(ss("wide_free"), 2 + 8)
        with nc.allow_non_contiguous_dma(reason="thirty columns of each channel"):
            pool.dma_start(conv_p, uT[:, :, HIST + SEQ - HIST:HIST + SEQ]).then_inc(ss("conv_out1"), 16)
            pool.dma_start(conv_s, uT[:, :, UCOLS - HIST:UCOLS]).then_inc(ss("conv_out1"), 16)
        pool.wait_ge(ss("kv_out"), 2 * HEADS)
        pool.dma_start(ret_p.rearrange("h p c -> p h c"), ret_out[:]).then_inc(ss("ret_p_out"), 16)
        pool.wait_ge(ss("state_new"), HEADS)
        pool.dma_start(ret_s.rearrange("h p c -> p h c"), rstate[:]).then_inc(ss("states_out"), 16)
        pool.wait_ge(ss("pe_done"), RET0 + 4)
        pool.dma_start(pT_raw[:], p_t).then_inc(ss("ple_in"), 16)
        pool.wait_ge(ss("m_ready"), 4)
        pool.dma_start(ln_gb[:], ln1.unsqueeze(0).broadcast_to([128, 2, D_MODEL])).then_inc(ss("ln1_in"), 16)
        pool.wait_ge(ss("h1_rows"), TILES)
        pool.dma_start(ln_gb[:], ln2.unsqueeze(0).broadcast_to([128, 2, D_MODEL])).then_inc(ss("ln2_in"), 16)

        def store_rows(n):
            pool.wait_ge(ss("y_ready"), n + 1)
            pool.dma_start(y_rows[ds(n * SLOTS, SLOTS), :], ysb[:]).then_inc(ss("y_stored"), 16)
            pool.wait_ge(ss("y_stored"), n * 16 + 16)
            pool.sem_inc(ss("y_free"), 1)

        with pool.Fori(0, EXPERTS) as n:
            store_rows(n)
        def gather_rows(count):
            pool.wait_ge(ss("pos_ready"), 1)
            for t in range(TILES):
                for k in range(2):
                    pool.indirect_dma_start(
                        out=yg[0:ROWS[t], k, t, :], out_offset=None, in_=y_rows[0:count, :],
                        in_offset=bass.IndirectOffsetOnAxis(ap=pos_u[0:ROWS[t], k, t:t + 1], axis=0),
                        bounds_check=count - 1).then_inc(y_got[t], 16)

        pool.wait_ge(ss("more_ready"), 1)
        flag = pool.value_load(more[0:1, 0:1], min_val=0, max_val=1)
        with pool.If(flag > 0):
            with pool.Fori(EXPERTS, EXPERTS * ROUNDS) as n:
                store_rows(n)
            gather_rows(ROUNDS * EXPERTS * SLOTS)
        with pool.Else():
            gather_rows(EXPERTS * SLOTS)

    @block.scalar
    def _(act):
        go = nc.scalar.activation

        def hi(i):
            act.wait_ge(raw_d_in[i % RAW_D], 16 * (i // RAW_D + 1))
            if i >= 2:
                act.wait_ge(ss("pe_done"), i - 1)
            go(whi[:, i % 2, :], raw_d[:, i % RAW_D, :], ACT.Copy).then_inc(ss("hi_ready"), 1)

        roots = [0]

        def root(t=None):
            roots[0] += 1
            act.wait_ge(ss("var_in"), roots[0])
            c = slice(0, TILES) if t is None else slice(t, t + 1)
            go(rstd[:, c], mv[:, c, 1], ACT.Sqrt).then_inc(ss("root_out"), 1)

        def hT_high(t):
            act.wait_ge(ss("hT_psum"), t + 1)
            go(hT[0][:, :, 128 * t:128 * t + ROWS[t]], rowsT_psum(t), ACT.Copy).then_inc(ss("hT_hi"), 1)

        for t in range(TILES):
            root(t)
        hT_high(0)
        hi(0)
        hT_high(1)
        hT_high(2)

        def head_copies(h):
            act.wait_ge(ss("heads_T"), h + 1)
            for w in range(2):
                go(qkT[:, h % 2, w, :], ps[:, 2 + w, 0:TOK], ACT.Copy).then_inc(ss("heads_copied"), 1)

        def state_copy(h):
            act.wait_ge(ss("kv_ready"), h + 1)
            go(ret_out[:, h, :], ps[:, 7, 0:DV], ACT.Copy).then_inc(ss("kv_out"), 1)
            if h >= 1:
                act.wait_ge(ss("state_new"), h)
            go(kv_s[:], ps[:, 7, DV:2 * DV], ACT.Copy).then_inc(ss("kv_out"), 1)

        SIGMOIDS_AT = {c + 1: (c,) for c in [*range(GA0, RET0), GB0, GB0 + 1]}
        SIGMOIDS_AT[GB0 + 5] = (GB0 + 2, GB0 + 3)

        def merged_high(c):
            act.wait_ge(ss("m_ready"), c + 1)
            go(mT[0][:, 2 * c:2 * c + 2, :], sA[:, 2 * c:2 * c + 2, :], ACT.Copy).then_inc(ss("m_hi_ready"), 1)

        def mid_part(t):
            act.wait_ge(ss("part_rest"), 2 * t + 1)
            go(h1b[:, 1, t], wide[:], ACT.Copy).then_inc(ss("part_mid"), 1)

        def last_part(t):
            act.wait_ge(ss("part_rest"), 2 * t + 2)
            go(h1b[:, 2, t], wide[:], ACT.Copy).then_inc(ss("part_last"), 1)

        def gate_sigmoids(b):
            act.wait_ge(ss("pe_done"), GATE0 + 2 * b + 2)
            for t in range(TILES):
                n = 3 * b + t
                if n >= 2:
                    act.wait_ge(ss("pe_mul"), n - 1)
                go(gate_sig[0:ROWS[t], n % 2, :], ps[0:ROWS[t], GATE_BANKS[b][t], :], ACT.Sigmoid).then_inc(ss("gate_sig_s"), 1)

        for i in range(DENSE):
            if i == 42:
                root(2)
                for t in range(TILES):
                    act.wait_ge(ss("h1T_psum"), t + 1)
                    go(h1T[0][:, :, 128 * t:128 * t + ROWS[t]], rowsT_psum(t), ACT.Copy).then_inc(ss("h1T_hi_s"), 1)
            if i:
                hi(i)
            if i == 41:
                root(0)
                root(1)
            if 1 <= i <= 8:
                act.wait_ge(ss("pe_done"), i)
                go(glu_sig[:, (i - 1) % 2, :], ps[:, 2 * ((i - 1) % 2) + 1, 0:TOK], ACT.Sigmoid).then_inc(ss("sig_ready"), 1)
            if i in (14, 16):
                b = (i - 10) // 2
                act.wait_ge(ss("pe_done"), i)
                for t in range(TILES):
                    go(vrow[0:ROWS[t], t, (b - 2) * 512:(b - 1) * 512], ps[0:ROWS[t], triple(b)[t], :], ACT.Copy).then_inc(ss("v_ready"), 1)
            if 2 <= i <= 9:
                if i == 2:
                    act.wait_ge(ss("conv_in"), 32)
                    act.wait_ge(ss("ident_in"), 16)
                    act.wait_ge(ss("h_rows"), TILES)
                for k in range(4 * (i - 2), min(4 * (i - 1), CONV_W)):
                    go(tap_diag[k], ident, ACT.Identity, scale=conv_par[:, 0, k:k + 1]).then_inc(ss("diag_ready"), 1)
            if i == 10:
                act.wait_ge(ss("conv0_psum"), 1)
                go(cT[:, 0, :], ps[:, 7, 0:CCOLS], ACT.Identity, bias=conv_par[:, 0, CONV_W:CONV_W + 1]).then_inc(ss("conv0_ready"), 1)
            if i == 16:
                head_copies(0)
            if 17 <= i <= 20:
                h = c = i - 1 - G0
                if h >= 1:
                    root()
                state_copy(h)
                if h + 1 < HEADS:
                    head_copies(h + 1)
                act.wait_ge(ss("pe_done"), i)
                go(gT[:, 2 * c:2 * c + 2, :], ps[:, 0:2, 0:TOK], ACT.Silu).then_inc(ss("wide_free"), 1)
            if i == 21:
                root()
            if i in (22, 23):
                for v in range(4 * (i - 22), 4 * (i - 22) + 4):
                    act.wait_ge(ss("at_ready"), v + 1)
                    go(AT[0][:, v, :], at_tmp[:, v % 2, :], ACT.Copy).then_inc(ss("at_hi"), 1)
            if i == 31:
                act.wait_ge(ss("cstd_ready"), 1)
                go(cstat[:], cstat[:], ACT.Sqrt).then_inc(ss("cstd_ready"), 1)
            for done in SIGMOIDS_AT.get(i, ()):
                c, w = (done - GA0, 12 + done - GA0) if done < GB0 else (done - GB0, 20 + done - GB0)
                act.wait_ge(ss("pe_done"), done + 1)
                act.wait_ge(ss("wide_free"), 2 + w)
                b = 2 * (done % 2)
                go((sA if done < GB0 else sB)[:, 2 * c:2 * c + 2, :], ps[:, b:b + 2, 0:TOK], ACT.Sigmoid).then_inc(ss("wide_free"), 1)
            if i in (31, 32, 33):
                for j in CT_PARTS[i - 31]:
                    act.wait_ge(ss("conv_norm"), j + 1)
                    go(cT[:, j, :], cT[:, j, :], ACT.Silu, bias=conv_par[:, j, CONV_W + 2:CONV_W + 3],
                       scale=conv_par[:, j, CONV_W + 1:CONV_W + 2]).then_inc(ss("silu_ready"), 1)
                    act.wait_ge(ss("silu_ready"), j + 1)
                    go(CT[0][:, j, :], cT[:, j, :], ACT.Copy).then_inc(ss("ct_hi"), 1)
            if i == 29:
                act.wait_ge(ss("conv_out1"), 32)
                for j in range(KT):
                    act.wait_ge(ss("centred"), j + 1)
                    go(sq[:, j, :], cT[:, j, :], ACT.Square).then_inc(ss("squared"), 1)
                act.wait_ge(ss("route_in"), 32)
                go(w_route_r[:, :, 0, :], w_route[:], ACT.Copy).then_inc(ss("route_hi"), 1)
            if i == 30:
                act.wait_ge(ss("ple_in"), 16)
                go(pT[0][:], pT_raw[:], ACT.Copy).then_inc(ss("pT_hi_s"), 1)
            if i == 33:
                for b in range(2):
                    act.wait_ge(ss("pe_done") if b else ss("proj_psum"), 33 if b else 1)
                    for t in range(TILES):
                        go(base_rows[0:ROWS[t], t, 512 * b:512 * b + 512], ps[0:ROWS[t], PROJ_BANKS[b][t], :], ACT.Copy).then_inc(ss("proj_evac"), 1)
            if 35 <= i <= 37:
                merged_high(i - 2 - CONV0)
            if i == 37:
                merged_high(3)
            if i == 42:
                go(h1b[:, 0], rows[:], ACT.Copy).then_inc(ss("part_hi"), 1)
                act.wait_ge(ss("logT_psum"), 1)
                go(logT[:], ps[0:72, 3, 0:TOK], ACT.Identity, bias=b_route[:]).then_inc(ss("logT_ready"), 1)
                mid_part(0)
                act.wait_ge(ss("gexp_in"), 1)
                go(r4[:], r4[:], ACT.Exp).then_inc(ss("gexp"), 1)
                act.wait_ge(ss("eexp_in"), 1)
                go(r1[:, 5, :], r1[:, 5, :], ACT.Exp).then_inc(ss("eexp"), 1)
                last_part(0)
                mid_part(1)
            if i == 43:
                last_part(1)
                mid_part(2)
            if i == 44:
                last_part(2)

        act.wait_ge(ss("lo_ready"), DENSE)

        def hi_x(r, e, j):
            slot, fills = raw_of(e, j)
            act.wait_ge(raw_x_in[slot], (fills + EXPERTS * r) * 16 + 16)
            c = chunk_of(r, e, j)
            if isinstance(e, int) and e == 0:
                if not isinstance(r, int):
                    act.wait_ge(ss("pe_done"), round_start(r))
                elif j == 3:
                    act.wait_ge(ss("pe_done"), DENSE - 1)
            elif isinstance(e, int) and e == 1 and j == 0:
                act.wait_ge(ss("pe_done"), round_start(r))
            elif isinstance(e, int) and e == 1:
                act.wait_ge(ss("pe_done"), chunk_of(r, 0, {1: 0, 3: 1, 4: 3}[j]) + 1)
            else:
                act.wait_ge(ss("pe_done"), c - 5)
            go(hi_slot[slot_of(e, j)], raw_x[slot][:], ACT.Copy).then_inc(ss("hi_ready"), 1)

        def x_high(n, done):
            act.wait_ge(ss("x_gathered"), n + 1)
            act.wait_ge(ss("pe_done"), done)
            go(xs[:, :, 0, :], ps[:, 7, :].rearrange("p (k s) -> p k s", k=KT), ACT.Copy).then_inc(ss("x_hi"), 1)

        def act_high(n):
            act.wait_ge(ss("act_T"), n + 1)
            go(aT[:, :, 0, :], ps[:, 3, :].rearrange("p (k s) -> p k s", k=4)[:, :, 0:SLOTS], ACT.Copy).then_inc(ss("act_hi"), 1)

        def y_copy(done):
            act.wait_ge(ss("pe_done"), done)
            go(ycp[:], ps[64:128, 4:6, :].rearrange("p a c -> p (a c)"), ACT.Copy).then_inc(ss("y_copied"), 1)

        def expert(r, e, first=False, second=False, last=False):
            n = r * EXPERTS + e
            c0 = chunk_of(r, e, 0)
            if not second:
                hi_x(r, e, 0)
                hi_x(r, e, 1)
            if first:
                if isinstance(r, int):
                    gate_sigmoids(0)
                x_high(n, round_start(r))
                if isinstance(r, int):
                    gate_sigmoids(1)
            elif not second:
                y_copy(c0)
            hi_x(r, e, 3)
            if not first:
                act_high(n - 1)
            act.wait_ge(ss("pe_done"), c0 + 2)
            go(gcp[:], ps[64:128, 1, :], ACT.Copy).then_inc(ss("gate_copied"), 1)
            if first:
                hi_x(r, 1, 0)
            else:
                hi_x(r, e, 4)
            act.wait_ge(ss("gate_summed"), n + 1)
            go(gsil[:], gsum[:], ACT.Silu).then_inc(ss("gate_silued"), 1)
            if first:
                hi_x(r, 1, 1)
            act.wait_ge(ss("pe_done"), c0 + 4)
            if not last:
                x_high(n + 1, c0 + 4)
            go(ucp[:], ps[64:128, 2, :], ACT.Copy).then_inc(ss("up_copied"), 1)

        def rounds(r):
            expert(r, 0, first=True)
            expert(r, 1, second=True)
            with act.Fori(2, EXPERTS - 1) as e:
                expert(r, e)
            expert(r, EXPERTS - 1, last=True)
            hi_x(r, EXPERTS, 0)
            c0 = chunk_of(r, EXPERTS, 0)
            y_copy(c0)
            act_high(r * EXPERTS + EXPERTS - 1)
            act.wait_ge(ss("y_ready"), r * EXPERTS + EXPERTS - 1)
            y_copy(c0 + 2)

        rounds(0)
        act.wait_ge(ss("more_ready"), 1)
        flag = act.value_load(more[0:1, 0:1], min_val=0, max_val=1)
        with act.If(flag > 0):
            with act.Fori(1, ROUNDS) as r:
                rounds(r)
        for t in range(TILES):
            for k in range(2):
                go(wdiag[:, t, k, :], ident, ACT.Identity, scale=wts[:, k, t:t + 1]).then_inc(ss("wdiag_ready"), 1)
        for t in range(TILES):
            root(t)

    @block.vector
    def _(dve):
        V = nc.vector
        tt, stt, ts = V.tensor_tensor, V.scalar_tensor_tensor, V.tensor_scalar
        link = Chain(dve, ss("dve_step"))

        def lo(i):
            dve.wait_ge(ss("hi_ready"), i + 1)
            tt(wlo[:, i % 2, :], raw_d[:, i % RAW_D, :], whi[:, i % 2, :].bitcast(F), ALU.subtract).then_inc(ss("lo_ready"), 1)

        roots = [0]

        def rows_begin(t, both=True, src=None):
            q = ROWS[t]
            for c in range(2) if both else (1,):
                link(V.bn_stats(stats[0:q, 2 * t + c, :], (rows[0:q, t, :] if src is None else src)[:, 512 * c:512 * c + 512]))
            link(V.bn_aggr(mv[0:q, t, :], stats[0:q, 2 * t:2 * t + 2, :]))
            ts(mv[:, t, 1:2], mv[:, t, 1:2], EPS, None, ALU.add).then_inc(ss("var_in"), 1)
            roots[0] += 1
            return roots[0]

        def layer_norm(gb, gb_in, out_sem, tmp, begin, after=lambda t: None, src=lambda t: rows[0:ROWS[t], t, :]):
            number = [begin(0), begin(1)]

            def finish(t):
                dve.wait_ge(ss("root_out"), number[t])
                link(V.reciprocal(rstd[:, t:t + 1], rstd[:, t:t + 1]))
                if t == 0:
                    dve.wait_ge(ss(gb_in), 16)
                norm_tile(t, gb, out_sem, tmp, src(t))

            finish(0)
            number.append(begin(2))
            finish(1)
            after(0)
            finish(2)
            after(1)
            after(2)

        def norm_tile(t, gb, out_sem, tmp, src):
            q = ROWS[t]
            if t:
                dve.wait_ge(ss(out_sem), t)
            link(stt(out=tmp[0:q, :], in0=src, scalar=mv[0:q, t, 0:1], in1=gb[0:q, 0, :],
                     op0=ALU.subtract, op1=ALU.mult))
            stt(out=rows[0:q, t, :], in0=tmp[0:q, :], scalar=rstd[0:q, t:t + 1], in1=gb[0:q, 1, :],
                op0=ALU.mult, op1=ALU.add).then_inc(ss(out_sem), 1)

        def merged_low(c):
            dve.wait_ge(ss("m_hi_ready"), c + 1)
            tt(mT[1][:, 2 * c:2 * c + 2, :], sA[:, 2 * c:2 * c + 2, :], mT[0][:, 2 * c:2 * c + 2, :].bitcast(F), ALU.subtract).then_inc(ss("m_lo_ready"), 1)

        def merge_in(blk, t):
            rr = rows[0:ROWS[t], t, 512 * blk:512 * blk + 512]
            stt(out=rr, in0=rr, scalar=ALPHA, in1=ps[0:ROWS[t], triple(blk)[t], :], op0=ALU.mult, op1=ALU.add).then_inc(ss("out_evac"), 1)

        def merge_begin(t):
            if t < 2:
                dve.wait_ge(ss("out_tile"), t + 1)
            else:
                dve.wait_ge(ss("pe_done"), OUT0 + 4)
            merge_in(1, t)
            dve.wait_ge(ss("out_evac"), 3 + t + 1)
            return rows_begin(t, both=False)

        def h1_low(t):
            dve.wait_ge(ss("h1T_hi_s"), t + 1)
            cols = slice(128 * t, 128 * t + ROWS[t])
            tt(h1T[1][:, :, cols], rowsT_psum(t), h1T[0][:, :, cols].bitcast(F), ALU.subtract).then_inc(ss("h1T_lo_s"), 1)

        def eps_root():
            roots[0] += 1
            ts(mv[:, :, 1], mv[:, :, 1], EPS, None, ALU.add).then_inc(ss("var_in"), 1)
            dve.wait_ge(ss("root_out"), roots[0])
            link(V.reciprocal(rstd[:], rstd[:]))

        V.memset(uT[:, :, 0:HIST], 0.0).then_inc(ss("row_free"), 6)
        V.memset(rows[64:128, 2, :], 0.0).then_inc(ss("wide_free"), 2)
        V.memset(rstd[:], 1.0).then_inc(ss("y_free"), 1)
        link(V.memset(mv[:], 1.0))
        def x_begin(t):
            dve.wait_ge(x_in[t], 16)
            return rows_begin(t)

        def h_low(t):
            dve.wait_ge(ss("hT_hi"), t + 1)
            cols = slice(128 * t, 128 * t + ROWS[t])
            tt(hT[1][:, :, cols], rowsT_psum(t), hT[0][:, :, cols].bitcast(F), ALU.subtract).then_inc(ss("hT_lo"), 1)
            if t == 0:
                lo(0)

        layer_norm(ln_in_gb, "ln_in_in", "h_rows", ln_tmp, x_begin, h_low)
        dve.wait_ge(ss("conv_in"), 32)
        dve.wait_ge(ss("const_in"), 32)

        TAPS_AT = {i: 6 for i in range(3, 9)}
        TAPS_AT.update({9: 42, 10: 5, 11: 1, 12: 5, 13: 1, 14: 12, 15: 11, 16: 10, 17: 5, 18: 7, 19: 7, 20: 7, 21: 5, 22: 4, 23: 6, 24: 11, 25: 10, 26: 9, 27: 6, 28: 400})
        taps = [(j, k, len(group)) for group in TAP_GROUPS for k in range(CONV_W) for j in group]
        n_taps = len(taps)

        def conv(count):
            for j, k, group in taps[:count]:
                n = n_taps - len(taps)
                if k:
                    dve.wait_ge(ss("taps_done"), n - group + 1)
                del taps[0]
                src, w = uT[:, j, k:k + CCOLS], conv_par[:, j, k:k + 1]
                if k == 0:
                    i = ts(cT[:, j, :], src, w, conv_par[:, j, CONV_W:CONV_W + 1], ALU.mult, ALU.add)
                else:
                    i = stt(out=cT[:, j, :], in0=src, scalar=w, in1=cT[:, j, :], op0=ALU.mult, op1=ALU.add)
                i.then_inc(ss("taps_done"), 1)

        def rotary(w, t):
            q, bank = ROWS[t], triple(w)[t]
            src = ps[0:q, bank, :].rearrange("p (h a d) -> p h a d", h=HEADS, a=2)
            cos = const[0:q, C_COS + 64 * t:C_COS + 64 * t + 64]
            sin = const[0:q, C_SIN + 64 * t:C_SIN + 64 * t + 64].unsqueeze(1).broadcast_to([q, HEADS, 64])
            cos8 = cos.unsqueeze(1).broadcast_to([q, 2 * HEADS, 64])
            A = rot[0:q, 0, :].rearrange("p (h a d) -> p h a d", h=HEADS, a=2)
            Bv = rot[0:q, 1, :].rearrange("p (h a d) -> p h a d", h=HEADS, a=2)
            out = qk[0:q, w, t, :].rearrange("p (h a d) -> p h a d", h=HEADS, a=2)
            tt(rot[0:q, 0, :].rearrange("p (g d) -> p g d", d=64), ps[0:q, bank, :].rearrange("p (g d) -> p g d", d=64), cos8, ALU.mult).then_inc(ss("dve_step"), 1)
            tt(Bv[:, :, 0, :], src[:, :, 1, :], sin, ALU.mult).then_inc(ss("dve_step"), 1)
            link.n += 2
            tt(Bv[:, :, 1, :], src[:, :, 0, :], sin, ALU.mult).then_inc(ss("row_free"), 1)
            dve.wait_ge(ss("dve_step"), link.n)
            dve.wait_ge(ss("row_free"), 6 + TILES * w + t + 1)
            tt(out[:, :, 0, :], A[:, :, 0, :], Bv[:, :, 0, :], ALU.subtract).then_inc(ss("qk_rows"), 1)
            tt(out[:, :, 1, :], A[:, :, 1, :], Bv[:, :, 1, :], ALU.add).then_inc(ss("qk_rows"), 1)
            dve.wait_ge(ss("qk_rows"), 2 * (TILES * w + t + 1))

        def head_scale(h):
            dve.wait_ge(ss("heads_T"), h + 1)
            for t in range(TILES):
                kr = qk[0:ROWS[t], 1, t, h * DK:(h + 1) * DK]
                ts(kr, kr, const[0:ROWS[t], C_ZETA + 4 * t + h:C_ZETA + 4 * t + h + 1], None, ALU.mult).then_inc(ss("kz_ready"), 1)
            dve.wait_ge(ss("heads_copied"), 2 * h + 1)
            tt(qx[:, h % 2, :], qkT[:, h % 2, 0, 256:320], const[:, C_XI + 64 * h:C_XI + 64 * h + 64], ALU.mult).then_inc(ss("q_scaled"), 1)

        def head_scores(h):
            dve.wait_ge(ss("scores"), h + 1)
            m = C_MASK + 448 * h
            tt(sT[:, h % 2, 0:384], ps[:, 4, 0:384], const[:, m:m + 384], ALU.mult).then_inc(ss("masked"), 1)
            tt(sT[0:64, h % 2, 384:448], ps[0:64, 4, 384:448], const[0:64, m + 384:m + 448], ALU.mult).then_inc(ss("masked"), 1)

        def head_norm(h):
            dve.wait_ge(ss("o_ready"), h + 1)
            dve.wait_ge(ss("kv_out"), 2 * h + 2)
            stt(out=rstate[:, h, :], in0=rstate[:, h, :], scalar=float(GAMMA[h] ** CHUNK), in1=kv_s[:],
                op0=ALU.mult, op1=ALU.add).then_inc(ss("state_new"), 1)
            o = [ps[:, 5, 0:DV], ps[:, 5, DV:2 * DV], ps[0:64, 6, 0:DV]]
            for t in range(TILES):
                link(V.bn_stats(stats[0:ROWS[t], t, :], o[t]))
                link(V.bn_aggr(mv[0:ROWS[t], t, :], stats[0:ROWS[t], t:t + 1, :]))
            eps_root()
            for t in range(TILES):
                ts(on[0:ROWS[t], t, h * DV:(h + 1) * DV], o[t], mv[0:ROWS[t], t, 0:1], rstd[0:ROWS[t], t:t + 1],
                   ALU.subtract, ALU.mult).then_inc(ss("on_ready"), 1)

        def at_mul(v):
            dve.wait_ge(ss("onT_psum"), v + 1)
            if v >= 2:
                dve.wait_ge(ss("at_lo"), v - 1)
            tt(at_tmp[:, v % 2, :], ps[:, 4 + v % 4, 0:TOK], gT[:, v, :], ALU.mult).then_inc(ss("at_ready"), 1)

        def at_low(v):
            dve.wait_ge(ss("at_hi"), v + 1)
            tt(AT[1][:, v, :], at_tmp[:, v % 2, :], AT[0][:, v, :].bitcast(F), ALU.subtract).then_inc(ss("at_lo"), 1)

        def bc(ap, shape):
            return ap.broadcast_to(shape)

        def first_max(values, prio, out, width, at_max):
            shape = [128, TILES, width]
            link(stt(out=out, in0=values, scalar=0.0, in1=bc(prio.unsqueeze(1), shape), op0=ALU.is_ge, op1=ALU.mult))
            link(V.tensor_reduce(r1[:, at_max, :], out, X, ALU.max))
            link(tt(out, out, bc(r1[:, at_max, :].unsqueeze(2), shape), ALU.is_equal))

        def route():
            red = V.tensor_reduce
            link(V.memset(logit[64:128, 2, :], 0.0))
            dve.wait_ge(ss("logit_psum"), 1)
            for t in range(TILES):
                link(V.tensor_copy(logit[0:ROWS[t], t, :], ps[0:ROWS[t], 7, 36 * t:36 * t + 36]))
            gl = logit[:, :, 0:GROUPS]
            link(red(r1[:, 0, :], gl, X, ALU.max))
            link(tt(r4[:], gl, bc(r1[:, 0, :].unsqueeze(2), [128, TILES, GROUPS]), ALU.subtract))
            first_max(r4[:], const[:, C_PRIO4:C_PRIO4 + 4], gsel[:], GROUPS, 1)
            V.memset(rankm[:, :, EXPERTS:EXPERTS + 1], -1.0).then_inc(ss("gexp_in"), 1)
            el = logit[:, :, GROUPS:].rearrange("p t (g e) -> p t g e", g=GROUPS)
            four = [128, TILES, GROUPS, PER_GROUP]

            def by_group(ap):
                return ap.rearrange("p t (g e) -> p t g e", g=GROUPS)

            gsel4 = bc(gsel[:].unsqueeze(3), four)
            link(tt(by_group(e32[:]), el, gsel4, ALU.mult))
            link(red(e8[:, 0], e32[:].rearrange("p t (g e) -> p t e g", g=GROUPS), X, ALU.add))
            eight = [128, TILES, PER_GROUP]
            link(red(r1[:, 3, :], e8[:, 0], X, ALU.max))
            link(tt(e8[:, 1], e8[:, 0], bc(r1[:, 3, :].unsqueeze(2), eight), ALU.subtract))
            first_max(e8[:, 1], const[:, C_PRIO8:C_PRIO8 + 8], s8[:, 0], PER_GROUP, 4)
            link(stt(out=e8[:, 1], in0=s8[:, 0], scalar=-BIG, in1=e8[:, 0], op0=ALU.mult, op1=ALU.add))
            link(red(r1[:, 6, :], e8[:, 1], X, ALU.max))
            tt(r1[:, 5, :], r1[:, 6, :], r1[:, 3, :], ALU.subtract).then_inc(ss("eexp_in"), 1)
            link(tt(e8[:, 0], e8[:, 1], bc(r1[:, 6, :].unsqueeze(2), eight), ALU.subtract))
            first_max(e8[:, 0], const[:, C_PRIO8:C_PRIO8 + 8], s8[:, 1], PER_GROUP, 7)
            for k in range(2):
                link(tt(by_group(sel[:, k]), gsel4, bc(s8[:, k].unsqueeze(2), four), ALU.mult))
            link(V.memset(sel[64:128, :, 2, :], 0.0))
            link(tt(taken[:], sel[:, 0], sel[:, 1], ALU.add))
            V.tensor_copy(taken16[:], taken[:]).then_inc(ss("taken_ready"), 1)
            dve.wait_ge(ss("gexp"), 1)
            link(red(r1[:, 2, :], r4[:], X, ALU.add))
            link(V.reciprocal(r1[:, 2, :], r1[:, 2, :]))
            dve.wait_ge(ss("eexp"), 1)
            link(ts(r1[:, 8, :], r1[:, 5, :], 1.0, None, ALU.add))
            link(V.reciprocal(r1[:, 8, :], r1[:, 8, :]))
            link(tt(wts[:, 0, :], r1[:, 8, :], r1[:, 2, :], ALU.mult))
            link(tt(wts[:, 1, :], wts[:, 0, :], r1[:, 5, :], ALU.mult))
            link(V.tensor_copy(iota[:], const[:, C_IOTA:C_IOTA + 64]))

        def ranks():
            dve.wait_ge(ss("rank_psum"), 1)
            link(V.tensor_copy(rank[:], ps[:, 7, 128:256].rearrange("p (t e) -> p t e", e=EXPERTS)))
            link(stt(out=rankm[:, :, 0:EXPERTS], in0=rank[:, 0:TILES, :], scalar=1.0, in1=taken[:], op0=ALU.add, op1=ALU.mult))
            link(ts(rankm[:, :, 0:EXPERTS], rankm[:, :, 0:EXPERTS], -1.0, None, ALU.add))
            pick(0, 0)

        def places():
            red = V.tensor_reduce
            rk = rank[:, 0:TILES, :]
            link(ts(e32[:], rk, float(SLOTS), None, ALU.is_ge))
            for j in range(2, ROUNDS):
                link(stt(out=e32[:], in0=rk, scalar=float(SLOTS * j), in1=e32[:], op0=ALU.is_ge, op1=ALU.add))
            link(stt(out=e32[:], in0=e32[:], scalar=float((EXPERTS - 1) * SLOTS), in1=rk, op0=ALU.mult, op1=ALU.add))
            link(tt(e32[:], e32[:], bc(const[:, C_EOFF:C_EOFF + EXPERTS].unsqueeze(1), [128, TILES, EXPERTS]), ALU.add))
            for k in range(2):
                link(tt(taken[:], sel[:, k], e32[:], ALU.mult))
                link(red(r1[:, 9 + k, :], taken[:], X, ALU.add))
            V.tensor_copy(pos_u[:], r1[:, 9:11, :]).then_inc(ss("pos_ready"), 1)
            link(red(r1[0:1, 11, 0:1], rank[0:1, TILES, :], X, ALU.max))
            ts(more[:], r1[0:1, 11, 0:1], float(SLOTS), None, ALU.is_gt).then_inc(ss("more_ready"), 1)

        def rest(t):
            if t == 0:
                dve.wait_ge(ss("part_hi"), 1)
            else:
                dve.wait_ge(ss("part_last"), t)
            tt(wide[:], rows[:, t, :], h1b[:, 0, t], ALU.subtract).then_inc(ss("part_rest"), 1)

        def rest_2(t):
            dve.wait_ge(ss("part_mid"), t + 1)
            dve.wait_ge(ss("part_rest"), 2 * t + 1)
            tt(wide[:], wide[:], h1b[:, 1, t], ALU.subtract).then_inc(ss("part_rest"), 1)

        def gates(b):
            for t in range(TILES):
                n = 3 * b + t
                q = ROWS[t]
                dve.wait_ge(ss("gate_sig_s"), n + 1)
                br = base_rows[0:q, t, 512 * b:512 * b + 512]
                tt(br, br, gate_sig[0:q, n % 2, :], ALU.mult).then_inc(ss("pe_mul"), 1)

        def pick(r, e):
            tt(onehot[:], iota[:].unsqueeze(1).broadcast_to([128, TILES, SLOTS]),
               rankm[:, :, ds(e, 1)].broadcast_to([128, TILES, SLOTS]), ALU.is_equal).then_inc(ss("onehot_ready"), 1)

        for i in range(DENSE):
            if i:
                lo(i)
            b = 2 * ((i - 1) % 2)
            if 1 <= i <= 8:
                dve.wait_ge(ss("sig_ready"), i)
                j = i - 1
                tt(uT[:, j, HIST:HIST + SEQ], ps[:, b, 0:SEQ], glu_sig[:, j % 2, 0:SEQ], ALU.mult).then_inc(ss("dve_step"), 1)
                link.n += 1
                tt(uT[:, j, S0 + HIST:UCOLS], ps[:, b, SEQ:TOK], glu_sig[:, j % 2, SEQ:TOK], ALU.mult).then_inc(ss("wide_free"), 1)
                dve.wait_ge(ss("dve_step"), link.n)
                dve.wait_ge(ss("wide_free"), 2 + i)
            if 10 <= i <= 13:
                w = (i - 10) // 2
                dve.wait_ge(ss("pe_done"), 10 + 2 * w)
                for t in (1, 2) if i % 2 else (0,):
                    rotary(w, t)
            if i == 16:
                head_scale(0)
            if 17 <= i <= 20:
                h = i - 17
                if h >= 1:
                    head_norm(h - 1)
                head_scores(h)
                if h + 1 < HEADS:
                    head_scale(h + 1)
            if i == 21:
                head_norm(3)
            if i in (22, 23):
                dve.wait_ge(ss("ret_p_out"), 16)
                first = 4 * (i - 22)
                at_mul(first)
                for v in range(first, first + 4):
                    if v + 1 < first + 4:
                        at_mul(v + 1)
                    at_low(v)
            if 25 <= i <= 28:
                c = i - 1 - RET0
                dve.wait_ge(ss("pe_done"), i)
                dve.wait_ge(ss("wide_free"), 2 + 16 + c)
                tt(sA[:, 2 * c:2 * c + 2, :], ps[:, b:b + 2, 0:TOK], sA[:, 2 * c:2 * c + 2, :], ALU.mult).then_inc(ss("wide_free"), 1)
            conv(TAPS_AT.get(i, 0))
            if i == 29:
                dve.wait_ge(ss("taps_done"), n_taps)
                dve.wait_ge(ss("mean_ready"), 1)
                for j in range(KT):
                    tt(cT[:, j, :], cT[:, j, :], ps[:, 7, 0:CCOLS], ALU.subtract).then_inc(ss("centred"), 1)
            if i == 30:
                dve.wait_ge(ss("route_hi"), 1)
                tt(w_route_r[:, :, 1, :], w_route[:], w_route_r[:, :, 0, :].bitcast(F), ALU.subtract).then_inc(ss("route_lo"), 1)
                dve.wait_ge(ss("pT_hi_s"), 1)
                tt(pT[1][:], pT_raw[:], pT[0][:].bitcast(F), ALU.subtract).then_inc(ss("pT_lo_s"), 1)
                dve.wait_ge(ss("var_ready"), 1)
                dve.wait_ge(ss("states_out"), 16)
                ts(cstat[:], ps[:, 7, 0:CCOLS], EPS, None, ALU.add).then_inc(ss("cstd_ready"), 1)
            if i == 31:
                dve.wait_ge(ss("cstd_ready"), 2)
                link(V.reciprocal(cstat[:], cstat[:]))
                for j in range(KT):
                    tt(cT[:, j, :], cT[:, j, :], cstat[:], ALU.mult).then_inc(ss("conv_norm"), 1)
            if i in (31, 32, 33):
                for j in CT_PARTS[i - 31]:
                    dve.wait_ge(ss("ct_hi"), j + 1)
                    tt(CT[1][:, j, :], cT[:, j, :], CT[0][:, j, :].bitcast(F), ALU.subtract).then_inc(ss("ct_lo"), 1)
            if 35 <= i <= 37:
                merged_low(i - 2 - CONV0)
            if 34 <= i <= 37:
                c = i - 1 - CONV0
                dve.wait_ge(ss("pe_done"), i)
                dve.wait_ge(ss("wide_free"), 2 + 24 + c)
                g = sB[:, 2 * c:2 * c + 2, :]
                tt(g[:, :, 0:SEQ], ps[:, b:b + 2, 0:SEQ], g[:, :, 0:SEQ], ALU.mult).then_inc(ss("dve_step"), 1)
                link.n += 1
                tt(g[:, :, SEQ:TOK], ps[:, b:b + 2, S0:CCOLS], g[:, :, SEQ:TOK], ALU.mult).then_inc(ss("wide_free"), 1)
                dve.wait_ge(ss("dve_step"), link.n)
                dve.wait_ge(ss("wide_free"), 2 + 24 + c + 1)
                tt(sA[:, 2 * c:2 * c + 2, :], sA[:, 2 * c:2 * c + 2, :], g, ALU.add).then_inc(ss("m_ready"), 1)
                if i == 37:
                    merged_low(3)
            if i == 39:
                dve.wait_ge(ss("pe_done"), i)
                for t in range(TILES):
                    merge_in(0, t)
                for t in range(TILES):
                    dve.wait_ge(ss("out_evac"), t + 1)
                    link(V.bn_stats(stats[0:ROWS[t], 2 * t, :], rows[0:ROWS[t], t, 0:512]))
            if i == 41:
                layer_norm(ln_gb, "ln1_in", "h1_rows", wide, merge_begin, h1_low)
            if i == 42:
                rest(0)
                route()
                rest_2(0)
                rest(1)
            if i == 43:
                rest_2(1)
                rest(2)
                ranks()
            if i == 44:
                rest_2(2)

        def alpha_h1():
            dve.wait_ge(ss("pe_mul"), 6)
            for t in range(TILES):
                q = ROWS[t]
                stt(out=base_rows[0:q, t, :], in0=rows[0:q, t, :], scalar=ALPHA, in1=base_rows[0:q, t, :],
                    op0=ALU.mult, op1=ALU.add).then_inc(ss("base_ready"), 1)

        def lo_x(r, e, j):
            dve.wait_ge(ss("hi_ready"), split_of(r, e, j) + 1)
            k = slot_of(e, j)
            tt(lo_slot[k], raw_x[raw_of(e, j)[0]][:], hi_slot[k].bitcast(F), ALU.subtract).then_inc(ss("lo_ready"), 1)

        def x_low(n):
            dve.wait_ge(ss("x_hi"), n + 1)
            tt(xs[:, :, 1, :], ps[:, 7, :].rearrange("p (k s) -> p k s", k=KT), xs[:, :, 0, :].bitcast(F), ALU.subtract).then_inc(ss("x_lo"), 1)

        def act_low(n):
            dve.wait_ge(ss("act_hi"), n + 1)
            tt(aT[:, :, 1, :], ps[:, 3, :].rearrange("p (k s) -> p k s", k=4)[:, :, 0:SLOTS], aT[:, :, 0, :].bitcast(F), ALU.subtract).then_inc(ss("act_lo"), 1)

        def y_sum(n):
            dve.wait_ge(ss("y_copied"), n + 1)
            dve.wait_ge(ss("y_free"), n + 1)
            tt(ysb[:], ps[0:64, 4:6, :].rearrange("p a c -> p (a c)"), ycp[:], ALU.add).then_inc(ss("y_ready"), 1)

        def expert(r, e, first=False, second=False, last=False):
            n = r * EXPERTS + e
            if not second:
                lo_x(r, e, 0)
                lo_x(r, e, 1)
            if first:
                if isinstance(r, int):
                    gates(0)
                x_low(n)
                if isinstance(r, int):
                    gates(1)
                pick(r, 1)
                if isinstance(r, int):
                    link(V.memset(act_rows[SLOTS:128, :], 0.0))
            elif not second:
                y_sum(n - 2)
            lo_x(r, e, 3)
            if not first:
                act_low(n - 1)
            if second and isinstance(r, int):
                places()
            dve.wait_ge(ss("gate_copied"), n + 1)
            tt(gsum[:], ps[0:64, 1, :], gcp[:], ALU.add).then_inc(ss("gate_summed"), 1)
            if first:
                lo_x(r, 1, 0)
                lo_x(r, 1, 1)
            else:
                lo_x(r, e, 4)
            if second and isinstance(r, int):
                alpha_h1()
            if not last:
                x_low(n + 1)
            dve.wait_ge(ss("up_copied"), n + 1)
            tt(usum[:], ps[0:64, 2, :], ucp[:], ALU.add).then_inc(ss("up_summed"), 1)
            dve.wait_ge(ss("gate_silued"), n + 1)
            dve.wait_ge(ss("up_summed"), n + 1)
            tt(act_rows[0:SLOTS, :], gsil[:], usum[:], ALU.mult).then_inc(ss("act_ready"), 1)
            if not last:
                pick(r, e + 2)

        def rounds(r):
            if not isinstance(r, int):
                ts(iota[:], iota[:], float(SLOTS), None, ALU.add).then_inc(ss("slots_moved"), 1)
                dve.wait_ge(ss("slots_moved"), r)
                pick(r, 0)
            expert(r, 0, first=True)
            expert(r, 1, second=True)
            with dve.Fori(2, EXPERTS - 1) as e:
                expert(r, e)
            expert(r, EXPERTS - 1, last=True)
            lo_x(r, EXPERTS, 0)
            y_sum(r * EXPERTS + EXPERTS - 2)
            act_low(r * EXPERTS + EXPERTS - 1)
            y_sum(r * EXPERTS + EXPERTS - 1)

        rounds(0)
        dve.wait_ge(ss("more_ready"), 1)
        flag = dve.value_load(more[0:1, 0:1], min_val=0, max_val=1)
        with dve.If(flag > 0):
            with dve.Fori(1, ROUNDS) as r:
                rounds(r)

        def y_begin(t):
            dve.wait_ge(ss("sum_psum"), t + 1)
            return rows_begin(t, src=sum_psum(t))

        layer_norm(ln_gb, "ln2_in", "final_rows", wide, y_begin, src=sum_psum)

    @block.tensor
    def _(pe):
        mm, tr = nc.tensor.matmul, nc.tensor.transpose

        def three(out, wh, wl, xh, xl, first, last):
            mm(out, wh, xh, start=first, stop=False)
            mm(out, wh, xl, start=False, stop=False)
            return mm(out, wl, xh, start=False, stop=last)

        def wide(c, par, src, cols, credit, banks=None):
            pe.wait_ge(ss("lo_ready"), c + 1)
            pe.wait_ge(ss("wide_free"), credit)
            w = [q[:, par, :].rearrange("p (k c) -> p k c", k=KT) for q in (whi, wlo)]
            for t in range(2):
                out = ps[:, (2 * par if banks is None else banks) + t, 0:cols]
                for k in range(KT):
                    m = three(out, w[0][:, k, 128 * t:128 * t + 128], w[1][:, k, 128 * t:128 * t + 128],
                              src[0][:, k, :], src[1][:, k, :], k == 0, k == KT - 1)
            m.then_inc(ss("pe_done"), 1)

        def row_half(c, par, src, banks, first, last, k0, tile_done=None):
            pe.wait_ge(ss("lo_ready"), c + 1)
            w = [q[:, par, :].rearrange("p (k c) -> p k c", k=4) for q in (whi, wlo)]
            for t in range(TILES):
                q = ROWS[t]
                out = ps[0:q, banks[t], :]
                for k in range(4):
                    xh, xl = (z[:, k0 + k, 128 * t:128 * t + q] for z in src)
                    mm(out, xh, w[0][:, k, :], start=first and k == 0, stop=False)
                    mm(out, xh, w[1][:, k, :], start=False, stop=False)
                    m = mm(out, xl, w[0][:, k, :], start=False, stop=last and k == 3)
                if tile_done and t + 1 < TILES:
                    m.then_inc(ss(tile_done), 1)
            m.then_inc(ss("pe_done"), 1)

        def transposed(out, src):
            for t in range(TILES):
                q = ROWS[t]
                m = tr(out[:, 128 * t:128 * t + q], src(t), ident[0:q, 0:q])
            return m

        def rows_T(t, ready, signal):
            q = ROWS[t]
            pe.wait_ge(ss(ready), t + 1)
            for k in range(KT):
                m = tr(rowsT_psum(t)[:, k, :], rows[0:q, t, 128 * k:128 * k + 128], ident[0:q, 0:q])
            m.then_inc(ss(signal), 1)

        def keep_warm(count, bank=3, zeros=False):
            w, v = (uT[:, 0, 0:HIST], uT[:, :, 0:HIST]) if zeros else (ident, const[:, 0:C_MASK])
            for _ in range(count):
                mm(ps[0:HIST if zeros else 128, bank, 0:KT * HIST if zeros else C_MASK], w, v, start=True, stop=True)

        pe.wait_ge(ss("row_free"), 6)
        keep_warm(WARM[0], zeros=True)
        pe.wait_ge(ss("ident_in"), 16)
        for t in range(TILES):
            rows_T(t, "h_rows", "hT_psum")
            keep_warm(WARM[1 + t])
        pe.wait_ge(ss("hT_lo"), TILES)
        with pe.Fori(0, 4) as n:
            for par in range(2):
                wide(n * 2 + par, par, hT, TOK, n * 2 + (par + 1))
        pe.wait_ge(ss("wide_free"), 2 + 1)
        pe.wait_ge(ss("conv_in"), 32)
        for k in range(CONV_W):
            pe.wait_ge(ss("diag_ready"), k + 1)
            m = mm(ps[:, 7, 0:CCOLS], tap_diag[k], uT[:, 0, k:k + CCOLS], start=k == 0, stop=k == CONV_W - 1)
        m.then_inc(ss("conv0_psum"), 1)
        with pe.Fori(0, 2) as n:
            for b in range(2):
                pe.wait_ge(ss("row_free"), n * 6 + (3 * b + 3))
                if b == 1:
                    pe.wait_ge(ss("wide_free"), 2 + 8)
                for half in range(2):
                    row_half(n * 4 + (QKV0 + 2 * b + half), half, hT, triple(b), half == 0, half == 1, 4 * half)

        def heads_T(h):
            for w in range(2):
                m = transposed(ps[:, 2 + w, :], lambda t: qk[0:ROWS[t], w, t, h * DK:(h + 1) * DK])
            m.then_inc(ss("heads_T"), 1)

        pe.wait_ge(ss("v_ready"), 2 * TILES)
        pe.wait_ge(ss("qk_rows"), 4 * TILES)
        pe.wait_ge(ss("state_in"), 16)
        heads_T(0)
        for h in range(HEADS):
            pe.wait_ge(ss("heads_copied"), 2 * (h + 1))
            if h >= 1:
                pe.wait_ge(ss("masked"), 2 * h)
            qT, kT = qkT[:, h % 2, 0, :], qkT[:, h % 2, 1, :]
            mm(ps[:, 4, 0:256], kT[:, 0:128], qT[:, 0:256], start=True, stop=True)
            mm(ps[:, 4, 256:384], kT[:, 128:256], qT[:, 128:256], start=True, stop=True)
            mm(ps[0:64, 4, 384:448], kT[:, 256:320], qT[:, 256:320], start=True, stop=True).then_inc(ss("scores"), 1)
            if h == 0:
                pe.wait_ge(ss("conv0_ready"), 1)
            pe.wait_ge(ss("kz_ready"), 3 * (h + 1))
            if h >= 1:
                pe.wait_ge(ss("kv_out"), 2 * h)
            v = [vrow[0:ROWS[t], t, h * DV:(h + 1) * DV] for t in range(TILES)]
            kz = [qk[0:ROWS[t], 1, t, h * DK:(h + 1) * DK] for t in range(TILES)]
            mm(ps[:, 7, 0:DV], kz[0], v[0], start=True, stop=False)
            mm(ps[:, 7, 0:DV], kz[1], v[1], start=False, stop=True)
            mm(ps[:, 7, DV:2 * DV], kz[2], v[2], start=True, stop=True).then_inc(ss("kv_ready"), 1)
            if h + 1 < HEADS:
                heads_T(h + 1)
            wide(G0 + h, h % 2, hT, TOK, 10 + h, banks=0)
            pe.wait_ge(ss("masked"), 2 * (h + 1))
            pe.wait_ge(ss("q_scaled"), h + 1)
            if h >= 1:
                pe.wait_ge(ss("on_ready"), 3 * h)
            sc = sT[:, h % 2, :]
            mm(ps[:, 5, 0:DV], sc[:, 0:128], v[0], start=True, stop=True)
            mm(ps[:, 5, DV:2 * DV], sc[:, 128:256], v[0], start=True, stop=False)
            mm(ps[:, 5, DV:2 * DV], sc[:, 256:384], v[1], start=False, stop=True)
            mm(ps[0:64, 6, 0:DV], sT[0:64, h % 2, 384:448], v[2], start=True, stop=False)
            mm(ps[0:64, 6, 0:DV], qx[:, h % 2, :], rstate[:, h, :], start=False, stop=True).then_inc(ss("o_ready"), 1)
        for c in range(4):
            wide(GA0 + c, c % 2, hT, TOK, 14 if c == 0 else 13 + c)
            if c < 2:
                pe.wait_ge(ss("on_ready"), 3 * HEADS)
                pe.wait_ge(ss("kv_out"), 2 * HEADS)
                if c:
                    pe.wait_ge(ss("at_ready"), 4)
                for v in range(4 * c, 4 * c + 4):
                    transposed(ps[:, 4 + v % 4, :], lambda t: on[0:ROWS[t], t, 128 * v:128 * v + 128]).then_inc(ss("onT_psum"), 1)
        pe.wait_ge(ss("at_lo"), KT)
        with pe.Fori(0, 2) as n:
            for par in range(2):
                wide(n * 2 + (RET0 + par), par, AT, TOK, n * 2 + (16 + par + 1))
        def mean(tiles):
            for j in tiles:
                if j:
                    pe.wait_ge(ss("taps_done"), CONV_W * max(g[-1] for g in TAP_GROUPS if g[0] <= j))
                else:
                    pe.wait_ge(ss("conv0_ready"), 1)
                m = mm(ps[:, 7, 0:CCOLS], meanw, cT[:, j, :], start=j == 0, stop=j == KT - 1)
            return m

        pe.wait_ge(ss("at_ready"), KT)
        mean(range(5))
        wide(GB0, 0, hT, TOK, 21)
        mean(range(5, KT)).then_inc(ss("mean_ready"), 1)
        wide(GB0 + 1, 1, hT, TOK, 22)
        pe.wait_ge(ss("centred"), KT)
        for j in range(KT):
            pe.wait_ge(ss("squared"), j + 1)
            m = mm(ps[:, 7, 0:CCOLS], meanw, sq[:, j, :], start=j == 0, stop=j == KT - 1)
        m.then_inc(ss("var_ready"), 1)
        wide(GB0 + 2, 0, hT, TOK, 23)
        wide(GB0 + 3, 1, hT, TOK, 24)
        pe.wait_ge(ss("lo_ready"), PROJ0 + 1)
        pe.wait_ge(ss("pT_lo_s"), 1)
        w = [q[:, PROJ0 % 2, :].rearrange("p (k c) -> p k c", k=2) for q in (whi, wlo)]
        for b in range(2):
            if b == 1:
                pe.wait_ge(ss("cstd_ready"), 1)
                pe.wait_ge(ss("wide_free"), 2 + 23)
            for t in range(TILES):
                q = ROWS[t]
                for k in range(2):
                    xh, xl = (z[:, k, 128 * t:128 * t + q] for z in pT)
                    out = ps[0:q, PROJ_BANKS[b][t], :]
                    mm(out, xh, w[0][:, k, 512 * b:512 * b + 512], start=k == 0, stop=False)
                    mm(out, xh, w[1][:, k, 512 * b:512 * b + 512], start=False, stop=False)
                    m = mm(out, xl, w[0][:, k, 512 * b:512 * b + 512], start=False, stop=k == 1)
            if b == 0:
                m.then_inc(ss("proj_psum"), 1)
        m.then_inc(ss("pe_done"), 1)
        pe.wait_ge(ss("ct_lo"), KT)
        for c in range(4):
            if c == 1:
                pe.wait_ge(ss("proj_evac"), 6)
            wide(CONV0 + c, (CONV0 + c) % 2, CT, CCOLS, 26 if c < 2 else 25 + c)
        for b in range(2):
            if b == 1:
                pe.wait_ge(ss("wide_free"), 2 + 28)
            for half in range(2):
                if b == 0:
                    pe.wait_ge(ss("m_lo_ready"), 2 + 2 * half)
                row_half(OUT0 + 2 * b + half, (OUT0 + half) % 2, mT, triple(b), half == 0, half == 1, 4 * half,
                         "out_tile" if b and half else None)
        for t in range(TILES):
            keep_warm(WARM[4 + t])
            rows_T(t, "h1_rows", "h1T_psum")
        keep_warm(WARM[7])
        pe.wait_ge(ss("route_lo"), 1)
        pe.wait_ge(ss("h1T_lo_s"), TILES)
        for k in range(KT):
            w = w_route_r[:, k, :, :].rearrange("p a c -> p (a c)")
            mm(ps[0:72, 3, 0:TOK], w, h1T[0][:, k, :], start=k == 0, stop=False)
            m = mm(ps[0:72, 3, 0:TOK], w, h1T[1][:, k, :], start=False, stop=k == KT - 1)
        m.then_inc(ss("logT_psum"), 1)

        def gate_chunk(b, half):
            row_half(GATE0 + 2 * b + half, (GATE0 + half) % 2, h1T, GATE_BANKS[b], half == 0, half == 1, 4 * half)

        pe.wait_ge(ss("logT_ready"), 1)
        for t in range(TILES):
            m = mm(ps[0:ROWS[t], 7, 36 * t:36 * t + 36], logT[:, 128 * t:128 * t + ROWS[t]], const[0:72, C_FOLD:C_FOLD + 36],
                   start=True, stop=True)
        m.then_inc(ss("logit_psum"), 1)
        gate_chunk(0, 0)
        pe.wait_ge(ss("taken_ready"), 1)
        for t in range(TILES + 1):
            n = min(t, TILES - 1)
            for f in range(n + 1):
                m = mm(ps[:, 7, 128 + 32 * t:160 + 32 * t], triu[:, 0 if t == f else 1, :], taken16[:, f, :],
                       start=f == 0, stop=f == n)
        m.then_inc(ss("rank_psum"), 1)

        def gather(r, e):
            pe.wait_ge(ss("onehot_ready"), r * (EXPERTS + 1) + e + 1)
            for k in range(KT):
                for part in range(3):
                    for t in range(TILES):
                        m = mm(ps[:, 7, SLOTS * k:SLOTS * k + SLOTS], h1b[:, part, t, 128 * k:128 * k + 128], onehot[:, t, :],
                               start=part == 0 and t == 0, stop=part == 2 and t == TILES - 1)
            m.then_inc(ss("x_gathered"), 1)

        gate_chunk(0, 1)
        gate_chunk(1, 0)
        gate_chunk(1, 1)
        pe.wait_ge(ss("part_last"), TILES)
        gather(0, 0)

        def product(r, e, j, stat, banks, k0, kts, first, last, whole=False):
            slot, fills = raw_of(e, j)
            if whole:
                pe.wait_ge(raw_x_in[slot], (fills + EXPERTS * r) * 16 + 16)
                parts = (raw_x[slot][:],)
            else:
                pe.wait_ge(ss("lo_ready"), split_of(r, e, j) + 1)
                parts = (hi_slot[slot_of(e, j)], lo_slot[slot_of(e, j)])
            for k in range(kts):
                rows_k = stat[:, k0 + k, :, :].rearrange("p a s -> p (a s)")
                for b in range(len(banks)):
                    for n, q in enumerate(parts):
                        wv = q.rearrange("p (k c) -> p k c", k=kts)
                        m = mm(ps[:, banks[b], :], rows_k.bitcast(F) if whole else rows_k, wv[:, k, 512 * b:512 * b + 512],
                               start=first and k == 0 and n == 0, stop=last and k == kts - 1 and n == len(parts) - 1)
            m.then_inc(ss("pe_done"), 1)

        def act_transposes(n):
            pe.wait_ge(ss("act_ready"), n + 1)
            for f in range(FF // 128):
                m = tr(ps[:, 3, 128 * f:128 * f + 128], act_rows[:, 128 * f:128 * f + 128], ident)
            m.then_inc(ss("act_T"), 1)

        def down(r, e, j0):
            pe.wait_ge(ss("act_lo"), r * EXPERTS + e)
            if not (isinstance(e, int) and e == 1):
                pe.wait_ge(ss("y_ready"), r * EXPERTS + e - 1)
            product(r, e, j0, aT, (4, 5), 0, 2, True, False)
            product(r, e, j0 + 1, aT, (4, 5), 2, 2, False, True, whole=True)

        def expert(r, e, first=False, last=False):
            n = r * EXPERTS + e
            pe.wait_ge(ss("x_lo"), n + 1)
            product(r, e, 0, xs, (1,), 0, 4, True, False)
            product(r, e, 1, xs, (1,), 4, 4, False, True)
            if not first:
                act_transposes(n - 1)
            if first and isinstance(r, int):
                pe.wait_ge(ss("gate_sig_s"), 6)
            product(r, e, 2, xs, (2,), 0, 4, True, False, whole=True)
            if not last:
                gather(r, e + 1)
            product(r, e, 3, xs, (2,), 4, 4, False, True)
            if not first:
                down(r, e, 4)

        def rounds(r):
            if not isinstance(r, int):
                gather(r, 0)
            expert(r, 0, first=True)
            with pe.Fori(1, EXPERTS - 1) as e:
                expert(r, e)
            expert(r, EXPERTS - 1, last=True)
            act_transposes(r * EXPERTS + EXPERTS - 1)
            keep_warm(WARM[9], bank=6)
            down(r, EXPERTS, 0)

        rounds(0)
        pe.wait_ge(ss("more_ready"), 1)
        flag = pe.value_load(more[0:1, 0:1], min_val=0, max_val=1)
        with pe.If(flag > 0):
            with pe.Fori(1, ROUNDS) as r:
                rounds(r)
        pe.wait_ge(ss("base_ready"), TILES)
        for t in range(TILES):
            q = ROWS[t]
            if t == 2:
                keep_warm(WARM[8], bank=6)
            for c in range(2):
                mm(sum_psum(t)[:, 512 * c:512 * c + 512], ident[0:q, 0:q], base_rows[0:q, t, 512 * c:512 * c + 512], start=True, stop=False)
        for t in range(TILES):
            q = ROWS[t]
            pe.wait_ge(ss("wdiag_ready"), 2 * t + 2)
            pe.wait_ge(y_got[t], 32)
            for k in range(2):
                for c in range(2):
                    m = mm(sum_psum(t)[:, 512 * c:512 * c + 512], wdiag[0:q, t, k, 0:q], yg[0:q, k, t, 512 * c:512 * c + 512],
                           start=False, stop=k == 1)
            m.then_inc(ss("sum_psum"), 1)

    block.__exit__(None, None, None)


def _wide(w, c):
    return w[:, 256 * c:256 * c + 256].reshape(KT, 128, 256).transpose(1, 0, 2).reshape(128, CH)


def _part(w, b, half):
    return w[512 * half:512 * half + 512, 512 * b:512 * b + 512].reshape(4, 128, 512).transpose(1, 0, 2).reshape(128, CH)


def _two_rows(w):
    return w.reshape(2, 128, 1024).transpose(1, 0, 2).reshape(128, CH)


def _stream(w_in, w_ret, w_conv, w_out, w_proj, w_gate, eg, eu, ed):
    out = np.empty((DENSE + PER_ROUND, 128, CH), w_in.dtype)
    a, b = w_in[:, 3072:4096], w_in[:, 4096:5120]
    for j in range(KT):
        pair = np.concatenate([a[:, 128 * j:128 * j + 128], b[:, 128 * j:128 * j + 128]], axis=1)
        out[GLU0 + j] = _wide(pair, 0)
    for blk in range(4):
        for half in range(2):
            out[QKV0 + 2 * blk + half] = _part(w_in[:, 0:2048], blk, half)
    for first, w in ((G0, w_in[:, 2048:3072]), (GA0, w_in[:, 5120:6144]), (RET0, w_ret), (GB0, w_in[:, 6144:7168]), (CONV0, w_conv)):
        for c in range(4):
            out[first + c] = _wide(w, c)
    for first, w in ((OUT0, w_out), (GATE0, w_gate)):
        for blk in range(2):
            for half in range(2):
                out[first + 2 * blk + half] = _part(w, blk, half)
    out[PROJ0] = _two_rows(w_proj)
    i = DENSE
    for e in range(EXPERTS + 1):
        if e < EXPERTS:
            for w in (eg[e], eu[e]):
                for half in range(2):
                    out[i] = _part(w, 0, half)
                    i += 1
        if e > 0:
            for half in range(2):
                out[i] = _two_rows(ed[e - 1][256 * half:256 * half + 256])
                i += 1
    return out


_OUTS = [("y", (TOK, D_MODEL)), ("ret_p", (HEADS, DK, DV)), ("ret_s", (HEADS, DK, DV)),
         ("conv_p", (128, KT, HIST)), ("conv_s", (128, KT, HIST))]


def kernel(**inputs):
    import ml_dtypes
    from concourse import bacc
    from concourse.bass_utils import run_bass_kernel_spmd

    i = {k: np.asarray(v) for k, v in inputs.items()}

    def by_channel(v):
        return np.moveaxis(v.reshape(*v.shape[:-1], KT, 128), (-1, -2), (0, 1))

    flat = lambda w: w.reshape(EXPERTS, *w.shape[-2:])
    t = np.arange(128)
    arrays = {
        "wstream": _stream(i["w_in"][0], i["w_ret_out"][0], i["w_conv_out"][0], i["w_out"][0], i["w_ple_proj"][0],
                           i["w_ple_gate"][0], flat(i["w_exp_gate"]), flat(i["w_exp_up"]), flat(i["w_exp_down"])),
        "x": np.concatenate([i["x_prompt"][0], i["x_sample"][0]]),
        "p_t": np.concatenate([i["p_prompt"][0, 0], i["p_sample"][0, 0]]).T.reshape(2, 128, TOK).transpose(1, 0, 2),
        "state_ret": i["state_ret"][0, 0],
        "state_conv": by_channel(i["state_conv"][0, 0]),
        "consts": _constants(),
        "triangle": np.stack([t[:, None] < t[None, :], np.ones((128, 128), bool)], axis=1).astype(ml_dtypes.bfloat16),
        "conv_params": np.concatenate([by_channel(i[n][0].reshape(-1, D_MODEL)) for n in ("conv_w", "conv_b", "conv_ln_g", "conv_ln_b")], axis=2),
        "route_w": np.concatenate([i["w_route_g"][0], *i["w_route_e"][0]], axis=1).reshape(KT, 128, 36).transpose(1, 0, 2),
        "route_b": np.concatenate([i["b_route_g"][0], i["b_route_e"][0].ravel(), np.zeros(36, np.float32)])[:, None],
        "ln_in": np.stack([i["ln_in_g"], i["ln_in_b"]]),
        "ln1": np.stack([i["ln1_g"][0], i["ln1_b"][0]]),
        "ln2": np.stack([i["ln2_g"][0], i["ln2_b"][0]]),
    }
    arrays = {k: np.ascontiguousarray(v) for k, v in arrays.items()}
    nc = bacc.Bacc("TRN2", target_bir_lowering=False, num_devices=1)
    args = [nc.dram_tensor(k, list(v.shape), mybir.dt.from_np(v.dtype), kind="ExternalInput").ap() for k, v in arrays.items()]
    args += [nc.dram_tensor(k, list(shape), mybir.dt.float32, kind="ExternalOutput").ap() for k, shape in _OUTS]
    _program(nc, *args)
    r = run_bass_kernel_spmd(nc, [arrays], core_ids=[0]).results[0]

    def history(v):
        return np.ascontiguousarray(np.asarray(v).transpose(2, 1, 0).reshape(1, 1, HIST, D_MODEL))

    yy = np.asarray(r["y"])
    return (yy[None, :SEQ], yy[None, SEQ:], np.asarray(r["ret_p"])[None, None], history(r["conv_p"]),
            np.asarray(r["ret_s"])[None, None], history(r["conv_s"]))
```
